# Optimizing a Trainium2 kernel written in Bass

```python
import math
import jax, jax.numpy as jnp
from jax import lax
import numpy as np
import jax
import jax.numpy as jnp

D_MODEL = 1024
BATCH = 1
SEQ = 256
DEPTH = 2

CTX_LEN = 256
GRID_W = 64
MLA_HEADS = 8
MLA_NOPE = 64
MLA_ROPE = 32
MLA_V = 64
MLA_QK = MLA_NOPE + MLA_ROPE
Q_LORA = 768
KV_LORA = 256
NA_HEADS = 8
NA_DIM = 64
NA_KH = 8
NA_KW = 16
D_FF = 4 * D_MODEL
N_BRANCH = 2
ROPE_BASE = 10000.0
ROPE_PAIRS = MLA_ROPE // 4
EPS = 1e-6
Q_BLOCK = 128
OFF_CQ = N_BRANCH * D_MODEL
OFF_CKV = OFF_CQ + Q_LORA
OFF_KR = OFF_CKV + KV_LORA
OFF_NA = OFF_KR + MLA_ROPE
IN_COLS = OFF_NA + 3 * NA_HEADS * NA_DIM


def rms_norm(x, g):
    xf = x.astype(jnp.float32)
    y = xf * lax.rsqrt(jnp.mean(xf * xf, axis=-1, keepdims=True) + EPS)
    return (y * g.astype(jnp.float32)).astype(x.dtype)

def modulate(h, shift, scale):
    return h * (1 + scale) + shift

def rope_half(x, ang):
    m = x.shape[-1] // 2
    x1, x2 = x[..., :m], x[..., m:]
    cos = jnp.cos(ang).astype(x.dtype)
    sin = jnp.sin(ang).astype(x.dtype)
    return jnp.concatenate([x1 * cos - x2 * sin, x1 * sin + x2 * cos], axis=-1)

def rope_2d(x, ang_r, ang_c):
    half = x.shape[-1] // 2
    return jnp.concatenate([rope_half(x[..., :half], ang_r), rope_half(x[..., half:], ang_c)], axis=-1)

def mixer_proj(h, w_in, g_qa, w_uq, g_kva, w_ukv, g_mq, g_mk, g_nq, g_nk):
    b_, s_ = h.shape[0], h.shape[1]
    p = h @ w_in
    gate_logits = p[..., :OFF_CQ]
    c_q = p[..., OFF_CQ:OFF_CKV]
    c_kv = p[..., OFF_CKV:OFF_KR]
    k_r = p[..., OFF_KR:OFF_NA]
    na = p[..., OFF_NA:].reshape(b_, s_, 3, NA_HEADS, NA_DIM)
    mq = (rms_norm(c_q, g_qa) @ w_uq).reshape(b_, s_, MLA_HEADS, MLA_QK)
    kv = (rms_norm(c_kv, g_kva) @ w_ukv).reshape(b_, s_, MLA_HEADS, MLA_NOPE + MLA_V)
    k_nope, mv = kv[..., :MLA_NOPE], kv[..., MLA_NOPE:]
    k_rope = jnp.broadcast_to(k_r[:, :, None, :], (b_, s_, MLA_HEADS, MLA_ROPE))
    mk = jnp.concatenate([k_nope, k_rope], axis=-1)
    mq = rms_norm(mq, g_mq)
    mk = rms_norm(mk, g_mk)
    nq = rms_norm(na[:, :, 0], g_nq)
    nk = rms_norm(na[:, :, 1], g_nk)
    nv = na[:, :, 2]
    return gate_logits, mq, mk, mv, nq, nk, nv

def dense_attention(q, k, v):
    scale = 1.0 / math.sqrt(q.shape[-1])
    s = jnp.einsum("bqhd,bkhd->bhqk", q, k).astype(jnp.float32) * scale
    p = jax.nn.softmax(s, axis=-1).astype(v.dtype)
    return jnp.einsum("bhqk,bkhe->bqhe", p, v)

def blocked_attention(q, k, v):
    b_, s_, h_, d_ = q.shape
    nb = s_ // Q_BLOCK
    qb = jnp.moveaxis(q.reshape(b_, nb, Q_BLOCK, h_, d_), 1, 0)
    ob = lax.map(lambda blk: dense_attention(blk, k, v), qb)
    return jnp.moveaxis(ob, 0, 1).reshape(b_, s_, h_, v.shape[-1])

def neighborhood_attention(q, k, v, k_ctx, v_ctx, rpb):
    b_, s_, h_, d_ = q.shape
    rows = s_ // GRID_W
    kh = min(NA_KH, rows)
    kw = NA_KW
    scale = 1.0 / math.sqrt(d_)
    to_grid = lambda t: t.reshape(b_, rows, GRID_W, h_, d_).transpose(1, 0, 3, 2, 4)
    q_g, k_g, v_g = to_grid(q), to_grid(k), to_grid(v)
    cols = jnp.arange(GRID_W)
    c_start = jnp.clip(cols - kw // 2, 0, GRID_W - kw)
    col_idx = c_start[:, None] + jnp.arange(kw)[None, :]
    dc_idx = col_idx - cols[:, None] + (NA_KW - 1)
    rpb_cols = rpb[:, :, dc_idx]

    def row_fn(args):
        q_r, r = args
        r_start = jnp.clip(r - kh // 2, 0, rows - kh)
        k_rows = lax.dynamic_slice_in_dim(k_g, r_start, kh, axis=0)
        v_rows = lax.dynamic_slice_in_dim(v_g, r_start, kh, axis=0)
        k_win = k_rows[:, :, :, col_idx]
        v_win = v_rows[:, :, :, col_idx]
        dr_idx = r_start + jnp.arange(kh) - r + (NA_KH - 1)
        bias = jnp.transpose(jnp.take(rpb_cols, dr_idx, axis=1), (0, 2, 1, 3))
        s_win = jnp.einsum("bhqd,ibhqjd->bhqij", q_r, k_win).astype(jnp.float32) * scale
        s_win = (s_win + bias.astype(jnp.float32)).reshape(b_, h_, GRID_W, kh * kw)
        s_ctx = jnp.einsum("bhqd,bkhd->bhqk", q_r, k_ctx).astype(jnp.float32) * scale
        p = jax.nn.softmax(jnp.concatenate([s_win, s_ctx], axis=-1), axis=-1).astype(v.dtype)
        p_win = p[..., :kh * kw].reshape(b_, h_, GRID_W, kh, kw)
        p_ctx = p[..., kh * kw:]
        return (jnp.einsum("bhqij,ibhqjd->bhqd", p_win, v_win)
                + jnp.einsum("bhqk,bkhd->bhqd", p_ctx, v_ctx))

    o = lax.map(row_fn, (q_g, jnp.arange(rows)))
    return o.transpose(1, 0, 3, 2, 4).reshape(b_, s_, h_ * d_)

def gated_merge(gate_logits, y_mla, y_na, w_mla_o, w_na_o, w_out):
    g = jax.nn.sigmoid(gate_logits.astype(jnp.float32)).astype(y_mla.dtype)
    y = g[..., :D_MODEL] * (y_mla @ w_mla_o) + g[..., D_MODEL:] * (y_na @ w_na_o)
    return y @ w_out

def squared_relu_mlp(h, w_ff1, w_ff2):
    return jnp.square(jax.nn.relu(h @ w_ff1)) @ w_ff2

def _normal(key, shape, scale):
    return jax.random.normal(key, shape, jnp.float32) * scale

def first_inputs(seed: int = 0) -> dict:
    key = jax.random.key(seed)
    ks = jax.random.split(key, 24)
    L = DEPTH
    gain = lambda k, n: 1.0 + _normal(k, (L, n), 0.1)
    return {
        "x": _normal(ks[0], (BATCH, SEQ, D_MODEL), 1.0),
        "c": _normal(ks[1], (BATCH, D_MODEL), 1.0),
        "ctx": _normal(ks[2], (BATCH, CTX_LEN, D_MODEL), 1.0),
        "c_ctx": _normal(ks[3], (D_MODEL,), 1.0),
        "w_ada": _normal(ks[4], (L, D_MODEL, 6 * D_MODEL), D_MODEL ** -0.5),
        "b_ada": _normal(ks[5], (L, 6 * D_MODEL), 0.02),
        "g_attn": gain(ks[6], D_MODEL),
        "w_in": _normal(ks[7], (L, D_MODEL, IN_COLS), D_MODEL ** -0.5),
        "g_qa": gain(ks[8], Q_LORA),
        "w_uq": _normal(ks[9], (L, Q_LORA, MLA_HEADS * MLA_QK), Q_LORA ** -0.5),
        "g_kva": gain(ks[10], KV_LORA),
        "w_ukv": _normal(ks[11], (L, KV_LORA, MLA_HEADS * (MLA_NOPE + MLA_V)), KV_LORA ** -0.5),
        "g_mla_q": gain(ks[12], MLA_QK),
        "g_mla_k": gain(ks[13], MLA_QK),
        "g_na_q": gain(ks[14], NA_DIM),
        "g_na_k": gain(ks[15], NA_DIM),
        "rpb": _normal(ks[16], (L, NA_HEADS, 2 * NA_KH - 1, 2 * NA_KW - 1), 0.1),
        "w_mla_o": _normal(ks[17], (L, MLA_HEADS * MLA_V, D_MODEL), (MLA_HEADS * MLA_V) ** -0.5),
        "w_na_o": _normal(ks[18], (L, NA_HEADS * NA_DIM, D_MODEL), (NA_HEADS * NA_DIM) ** -0.5),
        "w_out": _normal(ks[19], (L, D_MODEL, D_MODEL), D_MODEL ** -0.5),
        "g_mlp": gain(ks[20], D_MODEL),
        "w_ff1": _normal(ks[21], (L, D_MODEL, D_FF), D_MODEL ** -0.5),
        "w_ff2": _normal(ks[22], (L, D_FF, D_MODEL), D_FF ** -0.5),
    }

def first_block(x, c, ctx, c_ctx, w_ada, b_ada, g_attn, w_in, g_qa, w_uq, g_kva, w_ukv,
              g_mla_q, g_mla_k, g_na_q, g_na_k, rpb, w_mla_o, w_na_o, w_out,
              g_mlp, w_ff1, w_ff2):
    b_, s_, _ = x.shape
    l_ = ctx.shape[1]
    t = jnp.arange(s_)
    inv_freq = ROPE_BASE ** (-jnp.arange(ROPE_PAIRS, dtype=jnp.float32) / ROPE_PAIRS)
    ang_r = ((t // GRID_W).astype(jnp.float32)[:, None] * inv_freq)[:, None, :]
    ang_c = ((t % GRID_W).astype(jnp.float32)[:, None] * inv_freq)[:, None, :]
    silu_c = jax.nn.silu(c)
    silu_ctx = jax.nn.silu(c_ctx)
    x_lat, x_ctx = x, ctx
    for l in range(DEPTH):
        last = l == DEPTH - 1
        mod_lat = (silu_c @ w_ada[l] + b_ada[l])[:, None, :]
        mod_ctx = silu_ctx @ w_ada[l] + b_ada[l]
        sh1, sc1, gt1, sh2, sc2, gt2 = jnp.split(mod_lat, 6, axis=-1)
        csh1, csc1, cgt1, csh2, csc2, cgt2 = jnp.split(mod_ctx, 6, axis=-1)
        proj_w = (w_in[l], g_qa[l], w_uq[l], g_kva[l], w_ukv[l],
                  g_mla_q[l], g_mla_k[l], g_na_q[l], g_na_k[l])

        h_c = modulate(rms_norm(x_ctx, g_attn[l]), csh1, csc1)
        gl_c, mq_c, mk_c, mv_c, nq_c, nk_c, nv_c = mixer_proj(h_c, *proj_w)

        h = modulate(rms_norm(x_lat, g_attn[l]), sh1, sc1)
        gl, mq, mk, mv, nq, nk, nv = mixer_proj(h, *proj_w)
        mq = jnp.concatenate([mq[..., :MLA_NOPE], rope_2d(mq[..., MLA_NOPE:], ang_r, ang_c)], axis=-1)
        mk = jnp.concatenate([mk[..., :MLA_NOPE], rope_2d(mk[..., MLA_NOPE:], ang_r, ang_c)], axis=-1)
        y_mla = blocked_attention(mq, jnp.concatenate([mk_c, mk], axis=1),
                                  jnp.concatenate([mv_c, mv], axis=1)).reshape(b_, s_, MLA_HEADS * MLA_V)
        y_na = neighborhood_attention(nq, nk, nv, nk_c, nv_c, rpb[l])
        x_lat = x_lat + gt1 * gated_merge(gl, y_mla, y_na, w_mla_o[l], w_na_o[l], w_out[l])

        if not last:
            y_mla_c = dense_attention(mq_c, mk_c, mv_c).reshape(b_, l_, MLA_HEADS * MLA_V)
            y_na_c = dense_attention(nq_c, nk_c, nv_c).reshape(b_, l_, NA_HEADS * NA_DIM)
            x_ctx = x_ctx + cgt1 * gated_merge(gl_c, y_mla_c, y_na_c, w_mla_o[l], w_na_o[l], w_out[l])
            h2_c = modulate(rms_norm(x_ctx, g_mlp[l]), csh2, csc2)
            x_ctx = x_ctx + cgt2 * squared_relu_mlp(h2_c, w_ff1[l], w_ff2[l])

        h2 = modulate(rms_norm(x_lat, g_mlp[l]), sh2, sc2)
        x_lat = x_lat + gt2 * squared_relu_mlp(h2, w_ff1[l], w_ff2[l])
    return x_lat


N_MEM = 256
GROUP_WIDTH = 512
D_MIX = 4 * GROUP_WIDTH
NORM_EPS = 1e-6

RET_HEADS = 4
RET_HEAD_DIM = 128
RET_CHUNK = 128

SSD_HEADS = 8
SSD_HEAD_DIM = 64
SSD_GROUPS = 2
SSD_STATE = 128
SSD_CONV = 4
SSD_CHUNK = 128
SSD_BC = SSD_GROUPS * SSD_STATE
SSD_CONV_DIM = GROUP_WIDTH + 2 * SSD_BC
SSD_NORM_GROUP = GROUP_WIDTH // SSD_GROUPS
DT_MIN = 1e-3
DT_MAX = 1e-1
A_INIT_MIN = 1.0
A_INIT_MAX = 16.0

SB_HEADS = 4
SB_HEAD_DIM = 128
SB_BLOCK = 128

MEM_HEADS = 4
MEM_HEAD_DIM = 128

IN_SIZES = (GROUP_WIDTH, GROUP_WIDTH, GROUP_WIDTH, GROUP_WIDTH,
            SSD_CONV_DIM, GROUP_WIDTH, SSD_HEADS,
            GROUP_WIDTH, GROUP_WIDTH, GROUP_WIDTH, GROUP_WIDTH,
            GROUP_WIDTH, GROUP_WIDTH)
D_IN = sum(IN_SIZES)


def rmsnorm(x, g):
    xf = x.astype(jnp.float32)
    y = xf * lax.rsqrt(jnp.mean(xf * xf, axis=-1, keepdims=True) + NORM_EPS)
    return (y * g.astype(jnp.float32)).astype(x.dtype)

def apply_rope(t):
    s, d = t.shape[1], t.shape[-1]
    inv_freq = ROPE_BASE ** (-jnp.arange(0, d, 2, dtype=jnp.float32) / d)
    ang = jnp.arange(s, dtype=jnp.float32)[:, None] * inv_freq[None, :]
    cos = jnp.cos(ang)[None, :, None, :]
    sin = jnp.sin(ang)[None, :, None, :]
    t1, t2 = jnp.split(t.astype(jnp.float32), 2, axis=-1)
    return jnp.concatenate([t1 * cos - t2 * sin, t2 * cos + t1 * sin], axis=-1).astype(t.dtype)

def retention(q, k, v):
    b, s, h, d = q.shape
    dv = v.shape[-1]
    c = RET_CHUNK
    nc = s // c
    dt = v.dtype
    q = apply_rope(q)
    k = apply_rope(k) * (d ** -0.5)
    log_g = jnp.log(1.0 - 2.0 ** (-5.0 - jnp.arange(h, dtype=jnp.float32)))
    idx = jnp.arange(c, dtype=jnp.float32)
    rel = idx[:, None] - idx[None, :]
    intra = jnp.where(rel[None] >= 0, jnp.exp(rel[None] * log_g[:, None, None]), 0.0)
    zeta = jnp.exp((c - 1 - idx)[:, None] * log_g[None, :])
    xi = jnp.exp((idx + 1)[:, None] * log_g[None, :])
    chunk_decay = jnp.exp(c * log_g)
    qc = q.reshape(b, nc, c, h, d)
    kc = k.reshape(b, nc, c, h, d)
    vc = v.reshape(b, nc, c, h, dv)
    scores = jnp.einsum('bcnhd,bcmhd->bchnm', qc, kc) * intra.astype(dt)
    y_intra = jnp.einsum('bchnm,bcmhe->bcnhe', scores, vc)
    kv = jnp.einsum('bcmhd,bcmhe->bchde', kc * zeta.astype(dt)[:, :, None], vc)

    def step(state, kv_c):
        return chunk_decay[:, None, None] * state + kv_c, state

    _, r_prev = lax.scan(step, jnp.zeros((b, h, d, dv), jnp.float32),
                         jnp.moveaxis(kv.astype(jnp.float32), 1, 0))
    r_prev = jnp.moveaxis(r_prev, 0, 1).astype(dt)
    y_inter = jnp.einsum('bcnhd,bchde->bcnhe', qc, r_prev) * xi.astype(dt)[:, :, None]
    y = (y_intra + y_inter).reshape(b, s, h, dv).astype(jnp.float32)
    mu = jnp.mean(y, axis=-1, keepdims=True)
    var = jnp.mean(jnp.square(y - mu), axis=-1, keepdims=True)
    y = (y - mu) * lax.rsqrt(var + NORM_EPS)
    return y.reshape(b, s, h * dv).astype(dt)

def ssd_mixer(xbc, z, dt_raw, conv_w, conv_b, dt_bias, a_log, d_skip, norm_g):
    b, s, _ = xbc.shape
    dtype = xbc.dtype
    L = SSD_CHUNK
    nc = s // L
    G, J, P, N = SSD_GROUPS, SSD_HEADS // SSD_GROUPS, SSD_HEAD_DIM, SSD_STATE
    xbc = lax.conv_general_dilated(xbc, conv_w[:, None, :], window_strides=(1,),
                                   padding=[(SSD_CONV - 1, 0)],
                                   dimension_numbers=('NWC', 'WIO', 'NWC'),
                                   feature_group_count=SSD_CONV_DIM)
    xbc = jax.nn.silu(xbc + conv_b)
    xs, bm, cm = jnp.split(xbc, [GROUP_WIDTH, GROUP_WIDTH + SSD_BC], axis=-1)
    delta = jax.nn.softplus(dt_raw.astype(jnp.float32) + dt_bias.astype(jnp.float32))
    da = (delta * -jnp.exp(a_log.astype(jnp.float32))).reshape(b, nc, L, SSD_HEADS)
    x_heads = xs.reshape(b, s, SSD_HEADS, P)
    xdt = (x_heads * delta[..., None].astype(dtype)).reshape(b, nc, L, G, J, P)
    bc = bm.reshape(b, nc, L, G, N)
    cc = cm.reshape(b, nc, L, G, N)
    a_cs = jnp.cumsum(da, axis=2)
    causal = jnp.tril(jnp.ones((L, L), dtype=bool))[None, None, :, :, None]
    seg = a_cs[:, :, :, None, :] - a_cs[:, :, None, :, :]
    decay_in = jnp.exp(jnp.where(causal, seg, -jnp.inf)).reshape(b, nc, L, L, G, J)
    cb = jnp.einsum('bclgn,bcsgn->bclsg', cc, bc)
    y_diag = jnp.einsum('bclsgj,bcsgjp->bclgjp', cb[..., None] * decay_in.astype(dtype), xdt)
    decay_states = jnp.exp(a_cs[:, :, -1:, :] - a_cs).reshape(b, nc, L, G, J)
    states = jnp.einsum('bclgn,bclgjp->bcgjpn', bc, xdt * decay_states.astype(dtype)[..., None])
    chunk_decay = jnp.exp(a_cs[:, :, -1, :]).reshape(b, nc, G, J)

    def step(state, inp):
        dec, st = inp
        return dec[..., None, None] * state + st, state

    _, prev = lax.scan(step, jnp.zeros((b, G, J, P, N), jnp.float32),
                       (jnp.moveaxis(chunk_decay, 1, 0), jnp.moveaxis(states.astype(jnp.float32), 1, 0)))
    prev = jnp.moveaxis(prev, 0, 1).astype(dtype)
    y_off = jnp.einsum('bclgn,bcgjpn->bclgjp', cc, prev) * jnp.exp(a_cs).reshape(b, nc, L, G, J, 1).astype(dtype)
    y = (y_diag + y_off).reshape(b, s, SSD_HEADS, P) + x_heads * d_skip.astype(dtype)[:, None]
    y = y.reshape(b, s, GROUP_WIDTH) * jax.nn.silu(z)
    y = rmsnorm(y.reshape(b, s, SSD_GROUPS, SSD_NORM_GROUP), norm_g.reshape(SSD_GROUPS, SSD_NORM_GROUP))
    return y.reshape(b, s, GROUP_WIDTH)

def stick_breaking(q, k, v):
    b, s, h, d = q.shape
    nb = s // SB_BLOCK
    scale = d ** -0.5
    key_pos = jnp.arange(s)
    qb = jnp.moveaxis(q.reshape(b, nb, SB_BLOCK, h, d), 1, 0)

    def block(args):
        q_blk, i = args
        logits = jnp.einsum('bthd,bshd->bhts', q_blk, k).astype(jnp.float32) * scale
        q_pos = i * SB_BLOCK + jnp.arange(SB_BLOCK)
        causal = key_pos[None, :] < q_pos[:, None]
        log_beta = jax.nn.log_sigmoid(logits)
        log_1mb = jnp.where(causal, jax.nn.log_sigmoid(-logits), 0.0)
        tail = lax.cumsum(log_1mb, axis=3, reverse=True) - log_1mb
        w = jnp.where(causal, jnp.exp(log_beta + tail), 0.0)
        return jnp.einsum('bhts,bshd->bthd', w.astype(v.dtype), v)

    out = lax.map(block, (qb, jnp.arange(nb)))
    return jnp.moveaxis(out, 0, 1).reshape(b, s, h * d)

def memory_read(q, mem_n, w_mem_kv):
    b, s, h, d = q.shape
    kv = mem_n @ w_mem_kv
    k, v = jnp.split(kv, 2, axis=-1)
    k = k.reshape(b, -1, h, d)
    v = v.reshape(b, -1, h, d)
    logits = jnp.einsum('bshd,bmhd->bhsm', q, k).astype(jnp.float32) * (d ** -0.5)
    p = jax.nn.softmax(logits, axis=-1).astype(v.dtype)
    return jnp.einsum('bhsm,bmhd->bshd', p, v).reshape(b, s, h * d)

def hybrid_layer(x, mem, pre_g, post_g, w_in, conv_w, conv_b, dt_bias, a_log, d_skip,
                 ssd_norm_g, mem_norm_g, w_mem_kv, w_out):
    b, s, _ = x.shape
    hn = rmsnorm(x, pre_g)
    proj = hn @ w_in
    (ret_q, ret_k, ret_v, ret_g, xbc, z, dt_raw,
     sb_q, sb_k, sb_v, sb_g, mem_q, mem_g) = jnp.split(proj, list(np.cumsum(IN_SIZES)[:-1]), axis=-1)
    y_ret = retention(ret_q.reshape(b, s, RET_HEADS, RET_HEAD_DIM),
                      ret_k.reshape(b, s, RET_HEADS, RET_HEAD_DIM),
                      ret_v.reshape(b, s, RET_HEADS, RET_HEAD_DIM)) * jax.nn.silu(ret_g)
    y_ssd = ssd_mixer(xbc, z, dt_raw, conv_w, conv_b, dt_bias, a_log, d_skip, ssd_norm_g)
    y_sb = stick_breaking(sb_q.reshape(b, s, SB_HEADS, SB_HEAD_DIM),
                          sb_k.reshape(b, s, SB_HEADS, SB_HEAD_DIM),
                          sb_v.reshape(b, s, SB_HEADS, SB_HEAD_DIM)) * jax.nn.silu(sb_g)
    y_mem = memory_read(mem_q.reshape(b, s, MEM_HEADS, MEM_HEAD_DIM),
                        rmsnorm(mem, mem_norm_g), w_mem_kv) * jax.nn.silu(mem_g)
    y = jnp.concatenate([y_ret, y_ssd, y_sb, y_mem], axis=-1) @ w_out
    return x + rmsnorm(y, post_g)

def second_inputs(seed: int = 0) -> dict:
    key = jax.random.key(seed)
    ks = jax.random.split(key, 14)
    f32 = jnp.float32

    def gain(k, shape):
        return 1.0 + 0.02 * jax.random.normal(k, shape, f32)

    dt0 = jnp.exp(jax.random.uniform(ks[7], (DEPTH, SSD_HEADS), f32, math.log(DT_MIN), math.log(DT_MAX)))
    return {
        'x': jax.random.normal(ks[0], (BATCH, SEQ, D_MODEL), f32),
        'mem': jax.random.normal(ks[1], (BATCH, N_MEM, D_MODEL), f32),
        'pre_norm_g': gain(ks[2], (DEPTH, D_MODEL)),
        'post_norm_g': gain(ks[3], (DEPTH, D_MODEL)),
        'w_in': jax.random.normal(ks[4], (DEPTH, D_MODEL, D_IN), f32) * D_MODEL ** -0.5,
        'conv_w': jax.random.normal(ks[5], (DEPTH, SSD_CONV, SSD_CONV_DIM), f32) * SSD_CONV ** -0.5,
        'conv_b': 0.02 * jax.random.normal(ks[6], (DEPTH, SSD_CONV_DIM), f32),
        'dt_bias': dt0 + jnp.log(-jnp.expm1(-dt0)),
        'a_log': jnp.log(jax.random.uniform(ks[8], (DEPTH, SSD_HEADS), f32, A_INIT_MIN, A_INIT_MAX)),
        'd_skip': gain(ks[9], (DEPTH, SSD_HEADS)),
        'ssd_norm_g': gain(ks[10], (DEPTH, GROUP_WIDTH)),
        'mem_norm_g': gain(ks[11], (DEPTH, D_MODEL)),
        'w_mem_kv': jax.random.normal(ks[12], (DEPTH, D_MODEL, 2 * GROUP_WIDTH), f32) * D_MODEL ** -0.5,
        'w_out': jax.random.normal(ks[13], (DEPTH, D_MIX, D_MODEL), f32) * D_MIX ** -0.5,
    }

def second_block(x, mem, pre_norm_g, post_norm_g, w_in, conv_w, conv_b, dt_bias, a_log, d_skip,
              ssd_norm_g, mem_norm_g, w_mem_kv, w_out):
    for l in range(DEPTH):
        x = hybrid_layer(x, mem, pre_norm_g[l], post_norm_g[l], w_in[l], conv_w[l], conv_b[l],
                         dt_bias[l], a_log[l], d_skip[l], ssd_norm_g[l], mem_norm_g[l],
                         w_mem_kv[l], w_out[l])
    return x


def setup_inputs(seed=0):
    out = dict(first_inputs(seed))
    for name, value in second_inputs(seed + 1).items():
        if name != "x":
            out[name + "_2"] = value
    return out


def reference(
    x, c, ctx, c_ctx, w_ada, b_ada, g_attn, w_in, g_qa, w_uq, g_kva, w_ukv, g_mla_q, g_mla_k,
    g_na_q, g_na_k, rpb, w_mla_o, w_na_o, w_out, g_mlp, w_ff1, w_ff2, mem_2, pre_norm_g_2,
    post_norm_g_2, w_in_2, conv_w_2, conv_b_2, dt_bias_2, a_log_2, d_skip_2, ssd_norm_g_2,
    mem_norm_g_2, w_mem_kv_2, w_out_2,
):
    x = first_block(
        x, c, ctx, c_ctx, w_ada, b_ada, g_attn, w_in, g_qa, w_uq, g_kva, w_ukv, g_mla_q,
        g_mla_k, g_na_q, g_na_k, rpb, w_mla_o, w_na_o, w_out, g_mlp, w_ff1, w_ff2,
    )
    return second_block(
        x, mem_2, pre_norm_g_2, post_norm_g_2, w_in_2, conv_w_2, conv_b_2, dt_bias_2, a_log_2,
        d_skip_2, ssd_norm_g_2, mem_norm_g_2, w_mem_kv_2, w_out_2,
    )


_drawn_inputs = setup_inputs


def setup_inputs(seed=0):
    import zlib

    import numpy as np

    out = dict(_drawn_inputs(seed))
    spreads = {}
    factors = {'g_qa': 8.0,
     'g_mla_q': 8.0,
     'g_mla_k': 8.0,
     'g_na_q': 8.0,
     'g_na_k': 8.0,
     'rpb': 8.0,
     'pre_norm_g_2': 2.781,
     'post_norm_g_2': 4.782,
     'conv_b_2': 4.294,
     'd_skip_2': 200.0,
     'ssd_norm_g_2': 18.338,
     'mem_norm_g_2': 8.0}
    for name, (base, spread) in spreads.items():
        noise = np.random.default_rng([zlib.crc32(name.encode()), seed]).standard_normal(out[name].shape)
        drawn = base * np.exp(spread * noise) if base else spread * noise
        out[name] = jnp.asarray(drawn.astype(out[name].dtype))
    for name, factor in factors.items():
        out[name] = (out[name] * factor).astype(out[name].dtype)
    return out
```

```python
from contextlib import ExitStack

import numpy as np

import concourse.bass as bass
from concourse import mybir

F32 = mybir.dt.float32
ALU = mybir.AluOpType
ACT = mybir.ActivationFunctionType
AXX = mybir.AxisListType.X

P = 128
D, L, T, TC = 1024, 2, 256, 256
KT = D // P
TT = T + TC
QL, KVL, NH, NOPE, ROPE, VD = 768, 256, 8, 64, 32, 64
QK = NOPE + ROPE
ND = 64
FF = 4 * D
EPS = 1e-6
RING, SLOT = 5, 2048
BANKS = 8
W2 = 384
GRID, KW, KH = 64, 16, 8
NEG = -1e30

C_CQ, C_CKV, C_KR, C_NA = 2 * D, 2 * D + QL, 2 * D + QL + KVL, 2 * D + QL + KVL + ROPE
(O_RQ, O_RK, O_RV, O_RG, O_XBC, O_Z, O_DT, O_SQ, O_SK, O_SV, O_SG, O_MQ, O_MG, _) = np.cumsum(
    [0, 512, 512, 512, 512, 1024, 512, 8, 512, 512, 512, 512, 512, 512]).tolist()


def weight_entries():
    out = []

    def add(key, src, l, k0, nk, cols):
        out.append((key, src, l, k0, nk, cols))

    for l in range(L):
        for j in range(24):
            add(("ada", l, j), "w_ada", l, 0, KT, range(256 * j, 256 * j + 256))
        for i in range(6):
            add(("cq", l, i), "w_in", l, 0, KT, range(C_CQ + P * i, C_CQ + P * i + P))
        for i in range(2):
            add(("ckv", l, i), "w_in", l, 0, KT, range(C_CKV + P * i, C_CKV + P * i + P))
        add(("kr", l), "w_in", l, 0, KT, range(C_KR, C_KR + ROPE))
        for which, c0 in (("nq", C_NA), ("nk", C_NA + 512)):
            for i in range(4):
                add((which, l, i), "w_in", l, 0, KT, range(c0 + P * i, c0 + P * i + P))
        for i in range(2):
            add(("nv", l, i), "w_in", l, 0, KT, range(C_NA + 1024 + 256 * i, C_NA + 1280 + 256 * i))
        for h in range(NH):
            add(("uk", l, h), "w_ukv", l, 0, 2, range(P * h, P * h + NOPE))
        add(("uv", l), "w_ukv", l, 0, 2, [P * h + NOPE + e for h in range(NH) for e in range(VD)])
        for h in range(NH):
            add(("uq", l, h), "w_uq", l, 0, 6, range(QK * h, QK * h + QK))
        for n in range(KT):
            cols = range(P * n, P * n + P)
            add(("g1", l, n), "w_in", l, 0, KT, cols)
            add(("mo", l, n), "w_mla_o", l, 0, 4, cols)
            add(("no", l, n), "w_na_o", l, 0, 4, cols)
            add(("g2", l, n), "w_in", l, 0, KT, range(D + P * n, D + P * n + P))
        for n in range(KT):
            add(("out", l, n), "w_out", l, 0, KT, range(P * n, P * n + P))
        for n in range(FF // P):
            add(("ff1", l, n), "w_ff1", l, 0, KT, range(P * n, P * n + P))
        for n in range(KT):
            for half in range(2):
                add(("ff2", l, n, half), "w_ff2", l, 2048 * half, 16, range(P * n, P * n + P))
    for l in range(L):
        for i in range(4):
            add(("memk", l, i), "w_mem_kv_2", l, 0, KT, range(P * i, P * i + P))
        for i in range(2):
            add(("memv", l, i), "w_mem_kv_2", l, 0, KT, range(512 + 256 * i, 768 + 256 * i))
        add(("dt", l), "w_in_2", l, 0, KT, range(O_DT, O_DT + 8))
        for which, c0, n in (("xbc", O_XBC, 8), ("rq", O_RQ, 4), ("rk", O_RK, 4), ("sq", O_SQ, 4),
                             ("sk", O_SK, 4), ("mq", O_MQ, 4)):
            for i in range(n):
                add((which, l, i), "w_in_2", l, 0, KT, range(c0 + P * i, c0 + P * i + P))
        for which, c0 in (("rv", O_RV), ("sv", O_SV)):
            for i in range(2):
                add((which, l, i), "w_in_2", l, 0, KT, range(c0 + 256 * i, c0 + 256 * i + 256))
        for g, c0 in enumerate((O_RG, O_Z, O_SG, O_MG)):
            for i in range(4):
                add(("gate", l, 4 * g + i), "w_in_2", l, 0, KT, range(c0 + P * i, c0 + P * i + P))
        for n in range(KT):
            add(("out2", l, n), "w_out_2", l, 0, 16, range(P * n, P * n + P))
    return out


def weight_chunks():
    chunks, place = [], {}
    for e in weight_entries():
        size = e[4] * len(e[5])
        if not chunks or chunks[-1][1] + size > SLOT:
            chunks.append([[], 0])
        place[e[0]] = (len(chunks) - 1, chunks[-1][1], e[4], len(e[5]))
        chunks[-1][0].append(e)
        chunks[-1][1] += size
    return chunks, place


def columns(sizes):
    at, out = 0, {}
    for name, n in sizes:
        out[name] = (at, at + n)
        at += n
    return out, at


PARAMS, NPARAMS = columns([
    ("c", 16), ("b_ada", 96), ("g_attn", 16), ("g_mlp", 16), ("g_qa", 12), ("g_kva", 4),
    ("g_mla_q", 2), ("g_mla_k", 2), ("g_na_q", 2), ("g_na_k", 2),
    ("pre", 16), ("post", 16), ("mem", 16), ("ssd", 8), ("conv_w", 64), ("conv_b", 16),
    ("d_skip", 8), ("dt_bias", 16), ("a_log", 16)])
CONST, NCONST = columns([("ident", P), ("ones", P), ("pair", P), ("rot", ROPE), ("eps", 1), ("one", 1),
                         ("cos", T), ("sin", T)])
CONST2, NCONST2 = columns([("gt", P), ("le", 2 * P), ("ge", P), ("causal", W2), ("strict", W2),
                           ("neg", W2), ("decay", 4 * W2), ("cos", T), ("sin", T)])


def program(nc, dram, numbers):
    chunks, place = weight_chunks()
    ctx = ExitStack()
    with ctx:
        def sb(name, shape):
            return ctx.enter_context(nc.sbuf_tensor(name, shape, F32))

        sems, count, seen, rings, turn, freed = {}, {}, {}, {}, {}, {}

        def sem(name):
            if name not in sems:
                sems[name] = ctx.enter_context(nc.semaphore(name))
                count[name] = 0
            return sems[name]

        def signal(name, *key, by=1):
            s = sem(name)
            count[name] += by
            assert (name, *key) not in seen, (name, *key)
            seen[(name, *key)] = count[name]
            return s, by

        def event(name, *key):
            assert not numbers or (name, *key) in numbers, (name, *key)
            return sem(name), numbers.get((name, *key), 1)

        def buffers(ring_name, items):
            rings[ring_name], turn[ring_name], freed[ring_name] = items, 0, [None] * len(items)

        def take(eng, ring_name, key, until):
            s = turn[ring_name] % len(rings[ring_name])
            turn[ring_name] += 1
            if freed[ring_name][s] is not None:
                eng.wait_ge(*event(*freed[ring_name][s]))
            freed[ring_name][s] = until
            seen[("slot", ring_name, key)] = s
            return rings[ring_name][s]

        def given(ring_name, key):
            return rings[ring_name][numbers.get(("slot", ring_name, key), 0)]

        def bank(key):
            return given("bank", key)

        buffers("bank", [ctx.enter_context(nc.psum_tensor(f"bank{i}", [P, 512], F32)) for i in range(BANKS)])

        ring = sb("ring", [P, RING, SLOT])
        x = sb("x", [P, KT, TT])
        h = sb("h", [P, KT, TT])
        sq_all = sb("sq", [P, 4, TT])
        rs_all = sb("rs", [P, 2, TT])
        tmp_all = sb("tmp", [P, 4, TT])
        par = sb("par", [P, NPARAMS])
        con = sb("con", [P, NCONST])
        mod = sb("mod", [P, 48, 2])
        amp = sb("amp", [P, 2, KT, 2])
        silc = sb("silc", [P, 3, 16])
        gq = sb("gq", [P, 4])
        lowrank = sb("lowrank", [P, 4096])
        wide = sb("wide", [P, 16384])
        yT = sb("yT", [P, KT, TT])
        prob_all = sb("prob", [P, 3, TT])
        probT = sb("probT", [P, 2, 4, T])
        stat = sb("stat", [P, 4, 4])
        buffers("sq", [sq_all[:, i, :] for i in range(4)])
        buffers("rs", [rs_all[:, i, :] for i in range(2)])
        buffers("tmp", [tmp_all[:, i, :] for i in range(4)])
        buffers("prob", [prob_all[:, i, :] for i in range(3)])
        krope = prob_all

        def p(name, l=None):
            a, b = PARAMS[name]
            n = (b - a) // L if l is not None else b - a
            return par[:, a + (l or 0) * n:a + (l or 0) * n + n]

        def c(name):
            return con[:, CONST[name][0]:CONST[name][1]]

        ident, ones, pair, eps, one = c("ident"), c("ones"), c("pair"), c("eps"), c("one")
        ada_row = wide[0:2, 0:6144]
        cq = lowrank[:, 0:3072].rearrange("p (k t) -> p k t", k=6)
        ckv = lowrank[:, 3072:4096].rearrange("p (k t) -> p k t", k=2)
        bias = lowrank[:, :].rearrange("p (q h k) -> p q h k", q=2, h=NH)
        yg = lowrank[:, :].rearrange("p (k t) -> p k t", k=KT)
        mq = wide[:, 0:4096].rearrange("p (h t) -> p h t", h=NH)
        mk = wide[:, 4096:8192].rearrange("p (h t) -> p h t", h=NH)
        nq = wide[:, 8192:10240].rearrange("p (h t) -> p h t", h=4)
        nk = wide[:, 10240:12288].rearrange("p (h t) -> p h t", h=4)
        mv = wide[:, 12288:14336].rearrange("p (t e) -> p t e", t=4)
        nv = wide[:, 14336:16384].rearrange("p (t e) -> p t e", t=4)
        ff = wide[:, :].rearrange("p (n t) -> p n t", n=FF // P)
        heads1 = {"mq": mq, "mk": mk, "nq": nq, "nk": nk, "cq": cq, "ckv": ckv}

        x2 = x[:, :, TC:TT]
        h2 = h[:, :, 0:T]
        memn = h[:, :, T:TT]
        mem = wide[:, 0:2048].rearrange("p (k t) -> p k t", k=KT)
        conv_in = wide[:, 2048:2048 + 8 * T].rearrange("p (i t) -> p i t", i=8)
        at = 2048 + 8 * T
        xbc = wide[:, at:at + 2048].rearrange("p (i t) -> p i t", i=8)
        at += 2048
        heads2, vals2 = {}, {}
        for name in ("rq", "rk", "sq", "sk", "mq", "memk"):
            heads2[name] = wide[:, at:at + 1024].rearrange("p (h t) -> p h t", h=4)
            at += 1024
        for name in ("rv", "sv", "memv", "xs"):
            vals2[name] = wide[:, at:at + 1024].rearrange("p (t e) -> p t e", t=2)
            at += 1024
        assert at <= 16384
        gate = yT[:, :, :].rearrange("p k (a t) -> p (k a) t", a=2)
        yo = probT[:, :, :, :].rearrange("p a k t -> p (a k) t")
        du = prob_all[:, :, :].rearrange("p a t -> p (a t)")[:, 0:2 * W2].rearrange("p (a w) -> p a w", a=2)
        cbm = prob_all[:, :, :].rearrange("p a t -> p (a t)")[:, 2 * W2:4 * W2].rearrange("p (a w) -> p a w", a=2)
        rope_tmp = probT[:, 0, 0:2, :]
        work_all = probT[:, :, :, :].rearrange("p a k t -> p (a k t)")[:, 512:512 + 4 * W2]
        buffers("work", [work_all[:, W2 * i:W2 * i + W2] for i in range(4)])
        con2 = lowrank[:, 0:NCONST2]
        delta = lowrank[:, NCONST2:NCONST2 + 96].rearrange("p (a w) -> p a w", a=6)

        def y2(k):
            return x[:, k, 0:T] if k < 8 else conv_in[:, k - 8, :]

        def c2(name):
            return con2[:, CONST2[name][0]:CONST2[name][1]]

        def q0(l):
            return 0 if l == 0 else TC

        def groups(l):
            mla = lambda hd: (hd, slice(0, QK))
            na = lambda hd: (hd // 2, slice(ND * (hd % 2), ND * (hd % 2) + ND))
            out = [("mla", mq, mk, mv, mla, TC, 4, 0)]
            if l == 0:
                out.append(("mlac", mq, mk, mv, mla, 0, 2, 0))
            out.append(("na", nq, nk, nv, na, TC, 4, 4))
            if l == 0:
                out.append(("nac", nq, nk, nv, na, 0, 2, 4))
            return out

        block = ctx.enter_context(nc.Block())

        @block.tensor
        def _(pe):
            used = {"chunk": -1, "open": set()}

            def next_bank(*key, until):
                return take(pe, "bank", key, until)

            def weights(*key):
                i, off, nk, w = place[key]
                if i != used["chunk"]:
                    used["chunk"] = i
                    pe.wait_ge(*event(f"weights_in{i % RING}", i))
                used["open"].add(i)
                return ring[:, i % RING, off:off + nk * w].rearrange("p (k w) -> p k w", k=nk)

            def full(ins, *key):
                ins.then_inc(*signal("psum_full", *key))
                for i in used["open"]:
                    seen[("chunk_used", i)] = key
                used["open"] = set()

            def linear(out, w, src, ready=None, first=True, last=True):
                nk = w.shape[1]
                for k in range(nk):
                    if ready:
                        pe.wait_ge(*event(*ready, k))
                    mm = pe.matmul(out, w[:, k, :], src(k), start=first and k == 0, stop=last and k == nk - 1)
                return mm

            def sum_squares(name, l, n, w, stationary=ones):
                ps = next_bank("ss", name, l, until=("rs_log", name, l))
                for k in range(n):
                    pe.wait_ge(*event("squared", name, l, k))
                    mm = pe.matmul(ps[:, 0:w], stationary, given("sq", (name, l, k))[:, 0:w], start=k == 0, stop=k == n - 1)
                    if k < n - 1:
                        mm.then_inc(*signal("square_used", name, l, k))
                full(mm, "ss", name, l)

            def head_sum(name, i, l, w):
                if name in ("nq", "nk"):
                    return sum_squares((name, i), l, 1, w, pair)
                ps = next_bank("ss", (name, i), l, until=("rs_log", (name, i), l))
                s = given("sq", ((name, i), l, 0))
                pe.wait_ge(*event("squared", (name, i), l, 0))
                if name == "mk":
                    pe.matmul(ps[0:QK, 0:w], ones[0:NOPE, 0:QK], s[0:NOPE, 0:w], start=True, stop=False)
                    pe.wait_ge(*event("kr_squared", l))
                    mm = pe.matmul(ps[0:QK, 0:w], ones[NOPE:QK, 0:QK], krope[NOPE:QK, 1, TT - w:TT], start=False, stop=True)
                else:
                    mm = pe.matmul(ps[0:QK, 0:w], ones[0:QK, 0:QK], s[0:QK, 0:w], start=True, stop=True)
                full(mm, "ss", (name, i), l)

            def rotate(key, src, until):
                ps = next_bank(*key, until=until)
                mm = pe.matmul(ps[NOPE:QK, 0:T], c("rot")[NOPE:QK, :], src, start=True, stop=True)
                full(mm, *key)

            def values(name, l, lw, src, nk, tiles):
                for i in range(2):
                    for t in range(tiles):
                        w = weights(name, lw, i)
                        ps = next_bank(name, l, i, t, until=("v_copied", name, l, i, t))
                        for k in range(nk):
                            mm = pe.matmul(ps[:, 0:256], src(k)[:, P * t:P * t + P], w[:, k, :],
                                           start=k == 0, stop=k == nk - 1)
                        full(mm, name, l, i, t)

            def softmax_attention(g, n, nk, score, value, until="y_copied"):
                for u in range(n + 2):
                    if u < n:
                        ps = next_bank(g, "S", u, until=("exp", g, u))
                        full(score(ps, u), g, "S", u)
                    if u >= 2:
                        pe.wait_ge(*event("probs", g, u - 2))
                        ps = next_bank(g, "T", u - 2, until=("probT", g, u - 2))
                        for k in range(nk):
                            mm = pe.transpose(ps[:, P * k:P * k + P], given("prob", (g, u - 2))[:, P * k:P * k + P], ident)
                        full(mm, g, "T", u - 2)
                    if u >= 4 and u % 2 == 0:
                        one_value(g, u // 2 - 2, value, until)
                one_value(g, n // 2 - 1, value, until)

            def one_value(g, hd, value, until):
                pe.wait_ge(*event("probT", g, 2 * hd + 1))
                ps = next_bank(g, "Y", hd, until=(until, g, hd))
                full(value(ps, hd), g, "Y", hd)

            pe.wait_ge(*event("con_in"))

            for l in range(L):
                t0 = q0(l)
                cw = TT - t0
                pe.wait_ge(*event("silu_c"))
                for j in range(24):
                    w = weights("ada", l, j)
                    ps = next_bank("ada", l, j, until=("ada_copied", l, j))
                    for k in range(KT):
                        mm = pe.matmul(ps[0:2, 0:256], silc[:, 2, 2 * k:2 * k + 2], w[:, k, :],
                                       start=k == 0, stop=k == KT - 1)
                    full(mm, "ada", l, j)
                ps = next_bank("adaT", l, until=("mod", l))
                for n in range(48):
                    pe.wait_ge(*event("ada_copied", l, n // 2))
                    mm = pe.transpose(ps[:, 2 * n:2 * n + 2], ada_row[:, P * n:P * n + P], ident[0:2, 0:2])
                full(mm, "adaT", l)

                sum_squares("n1", l, KT, TT)
                for name, n, c0 in (("cq", 6, t0), ("ckv", 2, 0)):
                    for i in range(n):
                        ps = next_bank(name, l, i, until=("copied", name, l, i))
                        mm = linear(ps[:, 0:TT - c0], weights(name, l, i), lambda k: h[:, k, c0:TT], ("h", "n1", l))
                        full(mm, name, l, i)
                ps = next_bank("kr", l, 0, until=("copied", "kr", l, 0))
                full(linear(ps[NOPE:QK, :], weights("kr", l), lambda k: h[:, k, :]), "kr", l, 0)
                sum_squares("cq", l, 6, cw)
                sum_squares("ckv", l, 2, TT)
                for name, c0 in (("nq", t0), ("nk", 0)):
                    for i in range(5):
                        if i < 4:
                            ps = next_bank(name, l, i, until=("copied", name, l, i))
                            full(linear(ps[:, 0:TT - c0], weights(name, l, i), lambda k: h[:, k, c0:TT]), name, l, i)
                        if i:
                            head_sum(name, i - 1, l, TT - c0)
                values("nv", l, l, lambda k: h[:, k, :], KT, 4)
                pe.wait_ge(*event("kr_gain", l))
                rotate(("krot", l), krope[NOPE:QK, 2, TC:TT], ("krot_sin", l))
                for i in range(NH + 1):
                    if i < NH:
                        ps = next_bank("mk", l, i, until=("copied", "mk", l, i))
                        mm = linear(ps[0:NOPE, :], weights("uk", l, i), lambda k: ckv[:, k, :], ("normed", "ckv", l))
                        full(mm, "mk", l, i)
                    if i:
                        head_sum("mk", i - 1, l, TT)
                for t in range(4):
                    w = weights("uv", l)
                    ps = next_bank("mv", l, 0, t, until=("v_copied", "mv", l, 0, t))
                    for k in range(2):
                        mm = pe.matmul(ps[:, :], ckv[:, k, P * t:P * t + P], w[:, k, :], start=k == 0, stop=k == 1)
                    full(mm, "mv", l, 0, t)
                for i in range(NH + 2):
                    if i < NH:
                        ps = next_bank("mq", l, i, until=("copied", "mq", l, i))
                        mm = linear(ps[0:QK, 0:cw], weights("uq", l, i), lambda k: cq[:, k, t0:TT], ("normed", "cq", l))
                        full(mm, "mq", l, i)
                    if 0 < i <= NH:
                        head_sum("mq", i - 1, l, cw)
                    if i > 1:
                        pe.wait_ge(*event("normed", ("mq", i - 2), l, 0))
                        rotate(("qrot", l, i - 2), mq[NOPE:QK, i - 2, TC:TT], ("q_sin", l, i - 2))

                for gname, qs, ks, vs, rows, qcol, nk, _ in groups(l):
                    def score(ps, u):
                        a, r = rows(u // 2)
                        q = qcol + P * (u % 2)
                        if gname[:3] == "mla":
                            pe.wait_ge(*event("roped", "mq", l, u // 2))
                            pe.wait_ge(*event("k_ready", l, u // 2))
                        else:
                            pe.wait_ge(*event("normed", ("nk", 3), l, 0))
                        return pe.matmul(ps[:, 0:P * nk], qs[r, a, q:q + P], ks[r, a, 0:P * nk], start=True, stop=True)

                    def value(ps, hd):
                        for i, t in [(0, t) for t in range(4)] + ([(1, t) for t in range(4)] if gname[0] == "n" else []):
                            pe.wait_ge(*event("v_copied", "mv" if gname[0] == "m" else "nv", l, i, t))
                        r = VD * (hd % 2)
                        for k in range(nk):
                            mm = pe.matmul(ps[r:r + VD, 0:T], vs[:, k, VD * hd:VD * hd + VD],
                                           probT[:, hd % 2, k, :], start=k == 0, stop=k == nk - 1)
                        return mm

                    softmax_attention((gname, l), 2 * NH, nk, score, value)

                for g in groups(l):
                    pe.wait_ge(*event("y_copied", (g[0], l), NH - 1))
                for n in range(KT):
                    for name, src, by in (("g1", lambda k: h[:, k, t0:TT], "gate_exp"),
                                          ("mo", lambda k: yT[:, k, t0:TT], "merged"),
                                          ("no", lambda k: yT[:, 4 + k, t0:TT], "merged"),
                                          ("g2", lambda k: h[:, k, t0:TT], "gate_exp")):
                        ps = next_bank(name, l, n, until=(by, name, l, n))
                        full(linear(ps[:, 0:cw], weights(name, l, n), src), name, l, n)
                for n in range(KT):
                    ps = next_bank("out", l, n, until=("x_attn", l, n))
                    full(linear(ps[:, 0:cw], weights("out", l, n), lambda k: yg[:, k, t0:TT], ("yg", l)), "out", l, n)
                sum_squares("n2", l, KT, cw)
                for n in range(FF // P):
                    ps = next_bank("ff1", l, n, until=("relu", l, n))
                    mm = linear(ps[:, 0:cw], weights("ff1", l, n), lambda k: h[:, k, t0:TT], ("h", "n2", l))
                    full(mm, "ff1", l, n)
                for n in range(KT):
                    ps = next_bank("ff2", l, n, until=("x_mlp", l, n))
                    for half in range(2):
                        w = weights("ff2", l, n, half)
                        for k in range(16):
                            pe.wait_ge(*event("relu_squared", l, 16 * half + k))
                            mm = pe.matmul(ps[:, 0:cw], w[:, k, :], ff[:, 16 * half + k, t0:TT],
                                           start=half + k == 0, stop=half == 1 and k == 15)
                    full(mm, "ff2", l, n)

            sum_squares("mem", 2, KT, T)
            pe.wait_ge(*event("con2_in"))
            for lw in range(L):
                l = L + lw

                def tiles(name, n, src, ready, by):
                    for i in range(n):
                        ps = next_bank(name, l, i, until=(by, name, l, i))
                        full(linear(ps[:, 0:T], weights(name, lw, i), lambda k: src[:, k, :], ready), name, l, i)

                def causal_scores(key, by, ks, qs):
                    ps = next_bank(*key, until=by)
                    pe.matmul(ps[:, 0:T], ks[:, 0:P], qs, start=True, stop=True)
                    full(pe.matmul(ps[:, T:W2], ks[:, P:T], qs[:, P:T], start=True, stop=True), *key)

                def causal_product(ps, v, g, rows=slice(0, P)):
                    pe.matmul(ps[rows, 0:T], v[:, 0, :], g[:, 0:T], start=True, stop=False)
                    return pe.matmul(ps[rows, P:T], v[:, 1, :], g[:, T:W2], start=False, stop=True)

                tiles("memk", 4, memn, ("memn", l), "copied2")
                values("memv", l, lw, lambda k: memn[:, k, :], KT, 2)
                sum_squares("n3", l, KT, T)
                w = weights("dt", lw)
                ps = next_bank("dt", l, until=("dt_bias", l, 1))
                for t in range(2):
                    for k in range(KT):
                        pe.wait_ge(*event("h2", l, k))
                        mm = pe.matmul(ps[:, 8 * t:8 * t + 8], h2[:, k, P * t:P * t + P], w[:, k, :],
                                       start=k == 0, stop=k == KT - 1)
                full(mm, "dt", l)
                for name, n, by in (("xbc", 8, "copied"), ("rq", 4, "roped"), ("rk", 4, "roped"),
                                    ("sq", 4, "copied2"), ("sk", 4, "copied2"), ("mq", 4, "copied2")):
                    tiles(name, n, h2, ("h2", l), by)
                values("rv", l, lw, lambda k: h2[:, k, :], KT, 2)
                values("sv", l, lw, lambda k: h2[:, k, :], KT, 2)
                tiles("gate", 16, h2, ("h2", l), "gated_in")

                for t in range(2):
                    ps = next_bank("xsT", l, t, until=("v_copied", "xs", l, 0, t))
                    for i in range(4):
                        pe.wait_ge(*event("xbc", l, i))
                        mm = pe.transpose(ps[:, P * i:P * i + P], xbc[:, i, P * t:P * t + P], ident)
                    full(mm, "xsT", l, t)
                pe.wait_ge(*event("xbc", l, 7))
                for g in range(2):
                    causal_scores(("cb", l, g), ("cb_masked", l, g), xbc[:, 4 + g, :], xbc[:, 6 + g, :])

                def ssd_decay(hd):
                    pe.wait_ge(*event("du", l, hd))
                    ps = next_bank("seg", l, hd, until=("seg_exp", l, hd))
                    b = hd % 2
                    pe.matmul(ps[:, 0:T], du[:, b, 0:P], c2("le"), start=True, stop=False)
                    pe.matmul(ps[:, P:T], du[:, b, P:2 * P], c2("le")[:, 0:P], start=False, stop=True)
                    mm = pe.matmul(ps[:, T:W2], du[:, b, 2 * P:W2], c2("le")[:, 0:P], start=True, stop=True)
                    full(mm, "seg", l, hd)

                ssd_decay(0)
                for hd in range(8):
                    if hd < 7:
                        ssd_decay(hd + 1)
                    for t in range(2):
                        pe.wait_ge(*event("v_copied", "xs", l, 0, t))
                    pe.wait_ge(*event("ssd_g", l, hd))
                    if hd % 2 == 0:
                        ps_y = next_bank("ssdY", l, hd // 2, until=("ssd_skip", l, hd // 2))
                    mm = causal_product(ps_y, vals2["xs"][:, :, 64 * hd:64 * hd + 64], given("tmp", ("ssd_g", l, hd)),
                                        slice(64 * (hd % 2), 64 * (hd % 2) + 64))
                    full(mm, "ssdY", l, hd // 2) if hd % 2 else mm.then_inc(*signal("ssd_half", l, hd))
                for g in range(2):
                    sum_squares(("ssd", g), l, 2, T)

                def ret_scores(hd):
                    pe.wait_ge(*event("roped", "rk", l, hd))
                    causal_scores(("retS", l, hd), ("ret_decay", l, hd), heads2["rk"][:, hd, :], heads2["rq"][:, hd, :])

                ret_scores(0)
                for hd in range(4):
                    if hd < 3:
                        ret_scores(hd + 1)
                    for t in range(2):
                        pe.wait_ge(*event("v_copied", "rv", l, hd // 2, t))
                    pe.wait_ge(*event("ret_decay", l, hd))
                    ps = next_bank("retY", l, hd, until=("ret_y", l, hd))
                    mm = causal_product(ps, vals2["rv"][:, :, P * hd:P * hd + P], given("work", ("ret_decay", l, hd)))
                    full(mm, "retY", l, hd)
                for hd in range(4):
                    pe.wait_ge(*event("ret_y", l, hd))
                    ps = next_bank("retM", l, hd, until=("ret_centre", l, hd))
                    full(pe.matmul(ps[:, 0:T], ones, y2(hd), start=True, stop=True), "retM", l, hd)
                for hd in range(4):
                    sum_squares(("ret", hd), l, 1, T)

                def sb_scores(hd):
                    pe.wait_ge(*event("copied2", "sk", l, hd))
                    causal_scores(("sbS", l, hd), ("sb_logit", l, hd), heads2["sk"][:, hd, :], heads2["sq"][:, hd, :])

                def sb_value(hd):
                    for t in range(2):
                        pe.wait_ge(*event("v_copied", "sv", l, hd // 2, t))
                    pe.wait_ge(*event("sb_w", l, hd))
                    ps = next_bank("sbY", l, hd, until=("gated", l, 8 + hd))
                    mm = causal_product(ps, vals2["sv"][:, :, P * hd:P * hd + P], given("work", ("sb_logit", l, hd)))
                    full(mm, "sbY", l, hd)

                sb_scores(0)
                for hd in range(4):
                    if hd < 3:
                        sb_scores(hd + 1)
                    pe.wait_ge(*event("sb_softplus", l, hd))
                    ps = next_bank("sbT", l, hd, until=("sb_tail", l, hd))
                    s = given("sq", ("sb", l, hd))
                    pe.matmul(ps[:, 0:T], c2("ge"), s[:, 0:T], start=True, stop=False)
                    pe.matmul(ps[:, P:T], ones, s[:, T:W2], start=False, stop=True)
                    full(pe.matmul(ps[:, T:W2], c2("ge"), s[:, T:W2], start=True, stop=True), "sbT", l, hd)
                    if hd:
                        sb_value(hd - 1)
                sb_value(3)

                def mem_score(ps, u):
                    hd, qt = divmod(u, 2)
                    pe.wait_ge(*event("copied2", "mq", l, hd))
                    pe.wait_ge(*event("copied2", "memk", l, hd))
                    return pe.matmul(ps[:, 0:T], heads2["mq"][:, hd, P * qt:P * qt + P], heads2["memk"][:, hd, :],
                                     start=True, stop=True)

                def mem_value(ps, hd):
                    for k in range(2):
                        pe.wait_ge(*event("v_copied", "memv", l, hd // 2, k))
                        mm = pe.matmul(ps[:, 0:T], vals2["memv"][:, k, P * hd:P * hd + P], probT[:, hd % 2, k, :],
                                       start=k == 0, stop=k == 1)
                    return mm

                softmax_attention(("memory", l), 8, 2, mem_score, mem_value, "mem_gated")

                for k in range(12):
                    pe.wait_ge(*event("gated", l, k))
                pe.wait_ge(*event("mem_gated", ("memory", l), 3))
                for n in range(KT):
                    ps = next_bank("out2", l, n, until=("out_copied", l, n))
                    full(linear(ps[:, 0:T], weights("out2", lw, n), y2), "out2", l, n)
                sum_squares("n4", l, KT, T)

        @block.sync
        def _(sp):
            sp.dma_start(par[:, :], dram["par"]).then_inc(*signal("par_in", by=16))
            sp.dma_start(con[:, :], dram["con"]).then_inc(*signal("con_in", by=16))
            sp.dma_start(x[:, :, :], dram["x"]).then_inc(*signal("x_in", by=16))
            at = 0
            for i, (_, size) in enumerate(chunks):
                if i >= RING:
                    sp.wait_ge(*event("psum_full", *numbers.get(("chunk_used", i - RING), ("none",))))
                sp.dma_start(ring[:, i % RING, 0:size], dram["w"][at:at + P * size].rearrange("(p s) -> p s", p=P)).then_inc(*signal(f"weights_in{i % RING}", i, by=16))
                at += P * size
            sp.wait_ge(*event("x_out", 2 * L - 1, KT - 1))
            sp.dma_start(dram["out"], x2).then_inc(*signal("result_stored", by=16))
            sp.wait_ge(*event("result_stored"))

        @block.gpsimd
        def _(pool):
            for l in range(L):
                pool.wait_ge(*event("psum_full", "mq", l, NH - 1))
                pool.dma_start(bias[:, :, :, :], dram["bias"][l]).then_inc(*signal("bias_in", l, by=16))
            pool.wait_ge(*event("psum_full", "out", L - 1, KT - 1))
            pool.dma_start(con2, dram["con2"]).then_inc(*signal("con2_in", by=16))
            pool.wait_ge(*event("psum_full", "ff2", L - 1, KT - 1))
            pool.dma_start(mem, dram["mem"]).then_inc(*signal("mem_in", by=16))

        @block.scalar
        def _(act):
            def rms(name, l, n, rows, w, used):
                r = take(act, "rs", (name, l), used)[0:rows, 0:w]
                act.wait_ge(*event("psum_full", "ss", name, l))
                act.activation(r, bank(("ss", name, l))[0:rows, 0:w], ACT.Ln, bias=eps[0:rows, :], scale=1.0 / n).then_inc(*signal("rs_log", name, l))
                act.wait_ge(*event("rs_log", name, l))
                act.activation(r, r, ACT.Exp, scale=-0.5).then_inc(*signal("rs", name, l))

            def square(name, l, k, n, src, rows=slice(0, P)):
                until = ("square_used", name, l, k) if k < n - 1 else ("psum_full", "ss", name, l)
                s = take(act, "sq", (name, l, k), until)
                act.activation(s[rows, 0:src.shape[-1]], src, ACT.Square).then_inc(*signal("squared", name, l, k))

            def copy_values(name, l, i, t, dst, src_key):
                act.wait_ge(*event("psum_full", *src_key))
                act.activation(dst, bank(src_key)[:, 0:dst.shape[-1]], ACT.Copy).then_inc(*signal("v_copied", name, l, i, t))

            def softmax(g, n, w):
                for u in range(n + 2):
                    if u < n:
                        e = take(act, "prob", (g, u), ("psum_full", g, "T", u))
                        act.wait_ge(*event("neg_max", g, u))
                        act.activation(e[:, 0:w], bank((g, "S", u))[:, 0:w], ACT.Exp, bias=stat[:, u % 4, 0:1],
                                           accum_out=stat[:, u % 4, 1:2]).then_inc(*signal("exp", g, u))
                    if u >= 2:
                        v = u - 2
                        act.wait_ge(*event("psum_full", g, "T", v))
                        if v >= 4:
                            act.wait_ge(*event("psum_full", g, "Y", v // 2 - 2))
                        act.activation(probT[:, (v // 2) % 2, 0:w // P, P * (v % 2):P * (v % 2) + P],
                                           bank((g, "T", v))[:, 0:w].rearrange("p (k q) -> p k q", q=P), ACT.Copy).then_inc(*signal("probT", g, v))

            act.wait_ge(*event("par_in"))
            act.activation(silc[:, 0, :], p("c"), ACT.Exp, scale=-1.0).then_inc(*signal("c_exp"))
            act.wait_ge(*event("con_in"))
            act.wait_ge(*event("x_in"))

            for l in range(L):
                t0 = q0(l)
                cw = TT - t0

                def norm(name, c0, base):
                    for k in range(KT):
                        if name == "n2":
                            act.wait_ge(*event("x_attn", l, k))
                        elif l:
                            act.wait_ge(*event("x_mlp", l - 1, k))
                        square(name, l, k, KT, x[:, k, c0:TT])
                    rms(name, l, D, P, TT - c0, ("scaled", name, l, KT - 1))
                    for k in range(KT):
                        act.wait_ge(*event("scaled", name, l, k))
                        for s in ((1, 0) if c0 == 0 else (0,)):
                            cols = slice((1 - s) * TC, (1 - s) * TC + TC)
                            ins = act.activation(h[:, k, cols], h[:, k, cols], ACT.Identity,
                                                 bias=mod[:, base + k, s:s + 1])
                        ins.then_inc(*signal("h", name, l, k))

                for j in range(24):
                    act.wait_ge(*event("psum_full", "ada", l, j))
                    act.activation(ada_row[:, 256 * j:256 * j + 256], bank(("ada", l, j))[0:2, 0:256], ACT.Copy).then_inc(*signal("ada_copied", l, j))
                norm("n1", 0, 0)

                for name, n, c0 in (("cq", 6, t0), ("ckv", 2, 0)):
                    for i in range(n):
                        act.wait_ge(*event("copied", name, l, i))
                        square(name, l, i, n, heads1[name][:, i, c0:TT])
                act.wait_ge(*event("copied", "kr", l, 0))
                act.activation(krope[NOPE:QK, 1, :], krope[NOPE:QK, 0, :], ACT.Square).then_inc(*signal("kr_squared", l))
                rms("cq", l, QL, P, cw, ("normed", "cq", l, 5))
                rms("ckv", l, KVL, P, TT, ("normed", "ckv", l, 1))
                for name, c0 in (("nq", t0), ("nk", 0)):
                    for i in range(5):
                        if i < 4:
                            act.wait_ge(*event("copied", name, l, i))
                            square((name, i), l, 0, 1, heads1[name][:, i, c0:TT])
                        if i:
                            rms((name, i - 1), l, ND, P, TT - c0, ("normed", (name, i - 1), l, 0))
                for i in range(2):
                    for t in range(4):
                        copy_values("nv", l, i, t, nv[:, t, 256 * i:256 * i + 256], ("nv", l, i, t))
                for i in range(NH + 1):
                    if i < NH:
                        act.wait_ge(*event("copied", "mk", l, i))
                        square(("mk", i), l, 0, 1, mk[0:NOPE, i, :], slice(0, NOPE))
                    if i:
                        rms(("mk", i - 1), l, QK, QK, TT, ("k_ready", l, i - 1))
                for t in range(4):
                    copy_values("mv", l, 0, t, mv[:, t, :], ("mv", l, 0, t))
                for i in range(NH + 1):
                    if i < NH:
                        act.wait_ge(*event("copied", "mq", l, i))
                        square(("mq", i), l, 0, 1, mq[0:QK, i, t0:TT], slice(0, QK))
                    if i:
                        rms(("mq", i - 1), l, QK, QK, cw, ("normed", ("mq", i - 1), l, 0))

                for gname, _, _, _, _, _, nk, _ in groups(l):
                    softmax((gname, l), 2 * NH, P * nk)

                for n in range(KT):
                    for name, other in (("g1", "mo"), ("g2", "no")):
                        e = take(act, "tmp", (name, l, n), ("yg", l, n))
                        act.wait_ge(*event("psum_full", name, l, n))
                        act.activation(e[:, 0:cw], bank((name, l, n))[:, 0:cw], ACT.Exp, scale=-1.0).then_inc(*signal("gate_exp", name, l, n))
                norm("n2", t0, 24)
                for n in range(FF // P):
                    act.wait_ge(*event("relu", l, n))
                    act.activation(ff[:, n, t0:TT], ff[:, n, t0:TT], ACT.Square).then_inc(*signal("relu_squared", l, n))

            act.wait_ge(*event("mem_in"))
            for k in range(KT):
                square("mem", 2, k, KT, mem[:, k, :])
            rms("mem", 2, D, P, T, ("mem_normed", KT - 1))
            for lw in range(L):
                l = L + lw
                for i in range(4):
                    act.wait_ge(*event("psum_full", "memk", l, i))
                    act.activation(heads2["memk"][:, i, :], bank(("memk", l, i))[:, 0:T], ACT.Copy).then_inc(*signal("copied2", "memk", l, i))
                for i in range(2):
                    for t in range(2):
                        copy_values("memv", l, i, t, vals2["memv"][:, t, 256 * i:256 * i + 256], ("memv", l, i, t))
                for k in range(KT):
                    if lw:
                        act.wait_ge(*event("x_out", l - 1, k))
                    else:
                        act.wait_ge(*event("x_mlp", L - 1, k))
                    square("n3", l, k, KT, x2[:, k, :])
                rms("n3", l, D, P, T, ("h2", l, KT - 1))

                act.wait_ge(*event("dt_abs", l))
                act.activation(delta[:, 2, :], delta[:, 1, :], ACT.Exp).then_inc(*signal("dt_exp", l))
                act.wait_ge(*event("dt_exp", l))
                act.activation(delta[:, 3, :], delta[:, 2, :], ACT.Ln, bias=one).then_inc(*signal("dt_log", l))
                act.activation(delta[:, 5, 0:8], p("a_log", lw), ACT.Exp).then_inc(*signal("a_exp", l))
                for i in range(8):
                    e = take(act, "tmp", ("conv", l, i), ("xbc", l, i))
                    act.wait_ge(*event("conv", l, i))
                    act.activation(e[:, 0:T], xbc[:, i, :], ACT.Exp, scale=-1.0).then_inc(*signal("conv_exp", l, i))
                for name in ("sq", "sk", "mq"):
                    for i in range(4):
                        act.wait_ge(*event("psum_full", name, l, i))
                        act.activation(heads2[name][:, i, :], bank((name, l, i))[:, 0:T], ACT.Copy,
                                           scale=float(P) ** -0.5 if name == "mq" else 1.0).then_inc(*signal("copied2", name, l, i))
                for name in ("rv", "sv"):
                    for i in range(2):
                        for t in range(2):
                            copy_values(name, l, i, t, vals2[name][:, t, 256 * i:256 * i + 256], (name, l, i, t))
                for i in range(16):
                    e = take(act, "tmp", ("gate", l, i), ("gated_in", "gate", l, i))
                    act.wait_ge(*event("psum_full", "gate", l, i))
                    act.activation(e[:, 0:T], bank(("gate", l, i))[:, 0:T], ACT.Exp, scale=-1.0).then_inc(*signal("gate_exp2", l, i))
                for t in range(2):
                    copy_values("xs", l, 0, t, vals2["xs"][:, t, :], ("xsT", l, t))
                for hd in range(8):
                    e = take(act, "tmp", ("ssd_g", l, hd),
                                 ("psum_full", "ssdY", l, hd // 2) if hd % 2 else ("ssd_half", l, hd))
                    act.wait_ge(*event("psum_full", "seg", l, hd))
                    act.activation(e[:, 0:W2], bank(("seg", l, hd))[:, 0:W2], ACT.Exp).then_inc(*signal("seg_exp", l, hd))
                for g in range(2):
                    for k in range(2):
                        act.wait_ge(*event("ssd_gated", l, 2 * g + k))
                        square(("ssd", g), l, k, 2, y2(4 + 2 * g + k))
                    rms(("ssd", g), l, 256, P, T, ("gated", l, 5 + 2 * g))
                for hd in range(4):
                    act.wait_ge(*event("ret_centre", l, hd))
                    square(("ret", hd), l, 0, 1, y2(hd))
                for hd in range(4):
                    rms(("ret", hd), l, P, P, T, ("gated", l, hd))
                for hd in range(5):
                    if hd < 4:
                        s = take(act, "sq", ("sb", l, hd), ("psum_full", "sbT", l, hd))
                        s2 = given("work", ("sb_abs", l, hd))
                        act.wait_ge(*event("sb_abs", l, hd))
                        act.activation(s2[:, 0:W2], s2[:, 0:W2], ACT.Exp).then_inc(*signal("sb_exp", l, hd))
                        act.wait_ge(*event("sb_exp", l, hd))
                        act.activation(s[:, 0:W2], s2[:, 0:W2], ACT.Ln, bias=one).then_inc(*signal("sb_log", l, hd))
                    if hd:
                        z = given("work", ("sb_logit", l, hd - 1))[:, 0:W2]
                        act.wait_ge(*event("sb_tail", l, hd - 1))
                        act.activation(z, z, ACT.Exp).then_inc(*signal("sb_w", l, hd - 1))
                softmax(("memory", l), 8, T)
                for k in range(KT):
                    act.wait_ge(*event("out_copied", l, k))
                    square("n4", l, k, KT, yo[:, k, :])
                rms("n4", l, D, P, T, ("x_out", l, KT - 1))

        @block.vector
        def _(dve):
            steps = [0]

            def then(ins):
                steps[0] += 1
                ins.then_inc(*signal("vector_step", steps[0]))
                dve.wait_ge(*event("vector_step", steps[0]))

            def copy(name, l, i, dst, rows=slice(0, P)):
                dve.wait_ge(*event("psum_full", name, l, i))
                dve.tensor_copy(dst, bank((name, l, i))[rows, 0:dst.shape[-1]]).then_inc(*signal("copied", name, l, i))

            def scale_norm(name, l, k, dst, gain, rows, w, slot, last=True):
                dve.wait_ge(*event("rs", *slot))
                dve.scalar_tensor_tensor(dst, dst, gain, given("rs", slot)[rows, 0:w], ALU.mult, ALU.mult).then_inc(*signal("normed", name, l, k))

            def sigmoid(e):
                then(dve.tensor_scalar(e, e, 1.0, None, ALU.add))
                then(dve.reciprocal(e, e))

            def softmax(g, n, w, biased, y_out):
                for u in range(n + 5):
                    if u < n:
                        s = bank((g, "S", u))
                        dve.wait_ge(*event("psum_full", g, "S", u))
                        if biased:
                            hd, qt = divmod(u, 2)
                            then(dve.tensor_tensor(s[:, TC:TT], s[:, TC:TT], bias[:, qt, hd, :], ALU.add))
                        dve.tensor_reduce(stat[:, u % 4, 0:1], s[:, 0:w], AXX, ALU.max, negate=True).then_inc(*signal("neg_max", g, u))
                    if 1 <= u <= n:
                        v = u - 1
                        dve.wait_ge(*event("exp", g, v))
                        then(dve.reciprocal(stat[:, v % 4, 2:3], stat[:, v % 4, 1:2]))
                        e = given("prob", (g, v))[:, 0:w]
                        dve.tensor_scalar(e, e, stat[:, v % 4, 2:3], None, ALU.mult).then_inc(*signal("probs", g, v))
                    if u >= 5 and u % 2 == 1 and (u - 5) // 2 < n // 2:
                        y_out((u - 5) // 2)

            dve.wait_ge(*event("par_in"))
            dve.wait_ge(*event("c_exp"))
            then(dve.tensor_scalar(silc[:, 1, :], silc[:, 0, :], 1.0, None, ALU.add))
            then(dve.reciprocal(silc[:, 0, :], silc[:, 1, :]))
            dve.tensor_tensor(silc[:, 2, :], silc[:, 0, :], p("c"), ALU.mult).then_inc(*signal("silu_c"))
            for i, (name, n) in enumerate((("g_mla_q", QK), ("g_na_q", ND))):
                then(dve.tensor_scalar(gq[:, 2 * i:2 * i + 2], p(name), float(n) ** -0.5, None, ALU.mult))

            for l in range(L):
                t0 = q0(l)
                cw = TT - t0

                def norm(name, c0, which):
                    dve.wait_ge(*event("rs", name, l))
                    r = given("rs", (name, l))
                    for k in range(KT):
                        for s in ((1, 0) if c0 == 0 else (0,)):
                            cols = slice((1 - s) * TC, (1 - s) * TC + TC)
                            ins = dve.scalar_tensor_tensor(h[:, k, cols], x[:, k, cols], amp[:, which, k, s:s + 1],
                                                           r[:, cols.start - c0:cols.stop - c0], ALU.mult, ALU.mult)
                        ins.then_inc(*signal("scaled", name, l, k))

                dve.wait_ge(*event("psum_full", "adaT", l))
                ba = p("b_ada", l)
                a = bank(("adaT", l))[:, 0:96].rearrange("p (n s) -> p n s", s=2)
                for s in range(2):
                    ins = dve.tensor_tensor(mod[:, :, s], a[:, :, s], ba, ALU.add)
                ins.then_inc(*signal("mod", l))
                dve.wait_ge(*event("mod", l))
                for which, g in ((0, "g_attn"), (1, "g_mlp")):
                    for s in range(2):
                        at = 8 + 24 * which
                        then(dve.scalar_tensor_tensor(amp[:, which, :, s], mod[:, at:at + 8, s], 1.0, p(g, l),
                                                      ALU.add, ALU.mult))
                norm("n1", 0, 0)
                for name, n, c0 in (("cq", 6, t0), ("ckv", 2, 0)):
                    for i in range(n):
                        copy(name, l, i, heads1[name][:, i, c0:TT])
                dve.wait_ge(*event("psum_full", "kr", l, 0))
                dve.tensor_copy(krope[NOPE:QK, 0, :], bank(("kr", l, 0))[NOPE:QK, :]).then_inc(*signal("copied", "kr", l, 0))
                dve.wait_ge(*event("copied", "kr", l, 0))
                dve.tensor_scalar(krope[NOPE:QK, 2, :], krope[NOPE:QK, 0, :], p("g_mla_k", l)[NOPE:QK, :], None,
                                      ALU.mult).then_inc(*signal("kr_gain", l))
                for name, n, c0, g in (("cq", 6, t0, "g_qa"), ("ckv", 2, 0, "g_kva")):
                    for i in range(n):
                        scale_norm(name, l, i, heads1[name][:, i, c0:TT], p(g, l)[:, i:i + 1], slice(0, P), TT - c0, (name, l))
                for name, c0 in (("nq", t0), ("nk", 0)):
                    gain = gq[:, 2 + l:3 + l] if name == "nq" else p("g_na_k", l)
                    for i in range(5):
                        if i < 4:
                            copy(name, l, i, heads1[name][:, i, c0:TT])
                        if i:
                            dve.wait_ge(*event("squared", (name, i - 1), l, 0))
                            scale_norm((name, i - 1), l, 0, heads1[name][:, i - 1, c0:TT], gain, slice(0, P), TT - c0,
                                       ((name, i - 1), l))
                kr = krope[NOPE:QK, 2, TC:TT]
                e = krope[NOPE:QK, 0, 0:T]
                dve.wait_ge(*event("psum_full", "krot", l))
                dve.wait_ge(*event("kr_squared", l))
                dve.tensor_tensor(e, bank(("krot", l))[NOPE:QK, 0:T], c("sin")[NOPE:QK, :], ALU.mult).then_inc(*signal("krot_sin", l))
                then(dve.tensor_tensor(kr, kr, c("cos")[NOPE:QK, :], ALU.mult))
                dve.wait_ge(*event("krot_sin", l))
                then(dve.tensor_tensor(kr, kr, e, ALU.add))
                for i in range(NH + 1):
                    if i < NH:
                        copy("mk", l, i, mk[0:NOPE, i, :], slice(0, NOPE))
                    if i:
                        v = i - 1
                        dve.wait_ge(*event("rs", ("mk", v), l))
                        r = given("rs", (("mk", v), l))
                        dve.scalar_tensor_tensor(mk[0:NOPE, v, :], mk[0:NOPE, v, :], p("g_mla_k", l)[0:NOPE, :],
                                                 r[0:NOPE, :], ALU.mult, ALU.mult)
                        dve.tensor_tensor(mk[NOPE:QK, v, :], krope[NOPE:QK, 2, :], r[NOPE:QK, :], ALU.mult).then_inc(*signal("k_ready", l, v))
                for i in range(NH + 2):
                    if i < NH:
                        copy("mq", l, i, mq[0:QK, i, t0:TT], slice(0, QK))
                    if 0 < i <= NH:
                        v = i - 1
                        scale_norm(("mq", v), l, 0, mq[0:QK, v, t0:TT], gq[0:QK, l:l + 1], slice(0, QK), cw, (("mq", v), l))
                    if i > 1:
                        v = i - 2
                        e = krope[NOPE:QK, 0, T * (v % 2):T * (v % 2) + T]
                        q = mq[NOPE:QK, v, TC:TT]
                        dve.wait_ge(*event("psum_full", "qrot", l, v))
                        dve.tensor_tensor(e, bank(("qrot", l, v))[NOPE:QK, 0:T], c("sin")[NOPE:QK, :], ALU.mult).then_inc(*signal("q_sin", l, v))
                        then(dve.tensor_tensor(q, q, c("cos")[NOPE:QK, :], ALU.mult))
                        dve.wait_ge(*event("q_sin", l, v))
                        dve.tensor_tensor(q, q, e, ALU.add).then_inc(*signal("roped", "mq", l, v))

                for gname, _, _, _, _, qcol, nk, y0 in groups(l):
                    def y_out(hd):
                        r = slice(VD * (hd % 2), VD * (hd % 2) + VD)
                        dve.wait_ge(*event("psum_full", (gname, l), "Y", hd))
                        dve.tensor_copy(yT[r, y0 + hd // 2, qcol:qcol + T], bank(((gname, l), "Y", hd))[r, 0:T]).then_inc(*signal("y_copied", (gname, l), hd))

                    if gname == "na":
                        dve.wait_ge(*event("bias_in", l))
                    softmax((gname, l), 2 * NH, P * nk, gname == "na", y_out)

                for n in range(KT):
                    es = []
                    for name, other in (("g1", "mo"), ("g2", "no")):
                        e = given("tmp", (name, l, n))[:, 0:cw]
                        dve.wait_ge(*event("gate_exp", name, l, n))
                        sigmoid(e)
                        dve.wait_ge(*event("psum_full", other, l, n))
                        dve.tensor_tensor(e, e, bank((other, l, n))[:, 0:cw], ALU.mult).then_inc(*signal("merged", other, l, n))
                        es.append(e)
                    dve.wait_ge(*event("merged", "no", l, n))
                    dve.tensor_tensor(yg[:, n, t0:TT], es[0], es[1], ALU.add).then_inc(*signal("yg", l, n))

                def residual(name, done, base):
                    for n in range(KT):
                        dve.wait_ge(*event("psum_full", name, l, n))
                        for s in ((1, 0) if t0 == 0 else (0,)):
                            cols = slice((1 - s) * TC, (1 - s) * TC + TC)
                            ins = dve.scalar_tensor_tensor(
                                x[:, n, cols], bank((name, l, n))[:, cols.start - t0:cols.stop - t0],
                                mod[:, base + n, s:s + 1], x[:, n, cols], ALU.mult, ALU.add)
                        ins.then_inc(*signal(done, l, n))

                residual("out", "x_attn", 16)
                norm("n2", t0, 1)
                for n in range(FF // P):
                    dve.wait_ge(*event("psum_full", "ff1", l, n))
                    dve.tensor_scalar(ff[:, n, t0:TT], bank(("ff1", l, n))[:, 0:cw], 0.0, None, ALU.max).then_inc(*signal("relu", l, n))
                residual("ff2", "x_mlp", 40)

            dve.wait_ge(*event("rs", "mem", 2))
            for k in range(KT):
                dve.tensor_tensor(mem[:, k, :], mem[:, k, :], given("rs", ("mem", 2))[:, 0:T], ALU.mult).then_inc(*signal("mem_normed", k))
            dve.wait_ge(*event("con2_in"))
            for lw in range(L):
                l = L + lw
                dve.wait_ge(*event("mem_normed", KT - 1))
                for k in range(KT):
                    dve.tensor_scalar(memn[:, k, :], mem[:, k, :], p("mem", lw)[:, k:k + 1], None, ALU.mult).then_inc(*signal("memn", l, k))
                dve.wait_ge(*event("rs", "n3", l))
                for k in range(KT):
                    dve.scalar_tensor_tensor(h2[:, k, :], x2[:, k, :], p("pre", lw)[:, k:k + 1],
                                                 given("rs", ("n3", l))[:, 0:T], ALU.mult, ALU.mult).then_inc(*signal("h2", l, k))
                dve.wait_ge(*event("psum_full", "dt", l))
                for t in range(2):
                    dve.tensor_tensor(delta[:, 0, 8 * t:8 * t + 8], bank(("dt", l))[:, 8 * t:8 * t + 8],
                                          p("dt_bias", lw), ALU.add).then_inc(*signal("dt_bias", l, t))
                dve.wait_ge(*event("dt_bias", l, 1))
                dve.scalar_tensor_tensor(delta[:, 1, :], delta[:, 0, :], -1.0, delta[:, 0, :], ALU.mult, ALU.min).then_inc(*signal("dt_abs", l))

                def conv_silu(i):
                    e = given("tmp", ("conv", l, i))[:, 0:T]
                    dve.wait_ge(*event("conv_exp", l, i))
                    sigmoid(e)
                    dve.tensor_tensor(xbc[:, i, :], xbc[:, i, :], e, ALU.mult).then_inc(*signal("xbc", l, i))

                for i in range(9):
                    if i < 8:
                        dve.wait_ge(*event("psum_full", "xbc", l, i))
                        dve.tensor_copy(conv_in[:, i, :], bank(("xbc", l, i))[:, 0:T]).then_inc(*signal("copied", "xbc", l, i))
                        dve.wait_ge(*event("copied", "xbc", l, i))
                        taps = p("conv_w", lw)[:, 4 * i:4 * i + 4]
                        then(dve.tensor_scalar(xbc[:, i, :], conv_in[:, i, :], taps[:, 3:4],
                                               p("conv_b", lw)[:, i:i + 1], ALU.mult, ALU.add))
                        for j in range(1, 4):
                            ins = dve.scalar_tensor_tensor(xbc[:, i, j:T], conv_in[:, i, 0:T - j], taps[:, 3 - j:4 - j],
                                                           xbc[:, i, j:T], ALU.mult, ALU.add)
                            then(ins) if j < 3 else ins.then_inc(*signal("conv", l, i))
                    if i:
                        conv_silu(i - 1)
                for name in ("rq", "rk"):
                    for i in range(4):
                        ps = bank((name, l, i))
                        e = rope_tmp[:, i % 2, :]
                        dve.wait_ge(*event("psum_full", name, l, i))
                        dve.tensor_tensor(e[0:64, :], ps[64:P, 0:T], c2("sin")[64:P, :], ALU.mult)
                        dve.tensor_tensor(e[64:P, :], ps[0:64, 0:T], c2("sin")[0:64, :], ALU.mult)
                        then(dve.tensor_tensor(heads2[name][:, i, :], ps[:, 0:T], c2("cos"), ALU.mult))
                        dve.tensor_tensor(heads2[name][:, i, :], heads2[name][:, i, :], e, ALU.add).then_inc(*signal("roped", name, l, i))
                dve.wait_ge(*event("dt_log", l))
                then(dve.scalar_tensor_tensor(delta[:, 1, :], delta[:, 0, :], 0.0, delta[:, 3, :], ALU.max, ALU.add))
                dve.wait_ge(*event("a_exp", l))
                for t in range(2):
                    then(dve.scalar_tensor_tensor(delta[:, 4, 8 * t:8 * t + 8], delta[:, 1, 8 * t:8 * t + 8], -1.0,
                                                  delta[:, 5, 0:8], ALU.mult, ALU.mult))
                for i in range(16):
                    e = given("tmp", ("gate", l, i))[:, 0:T]
                    dve.wait_ge(*event("gate_exp2", l, i))
                    sigmoid(e)
                    dve.tensor_tensor(gate[:, i, :], e, bank(("gate", l, i))[:, 0:T], ALU.mult).then_inc(*signal("gated_in", "gate", l, i))

                for g in range(2):
                    dve.wait_ge(*event("psum_full", "cb", l, g))
                    dve.tensor_tensor(cbm[:, g, :], bank(("cb", l, g))[:, 0:W2], c2("causal"), ALU.mult).then_inc(*signal("cb_masked", l, g))

                def ssd_du(hd):
                    if hd >= 2:
                        dve.wait_ge(*event("psum_full", "seg", l, hd - 2))
                    b = hd % 2
                    dve.tensor_scalar(du[:, b, 0:P], c2("gt"), delta[:, 4, hd:hd + 1], None, ALU.mult)
                    dve.tensor_scalar(du[:, b, P:2 * P], ones, delta[:, 4, 8 + hd:9 + hd], None, ALU.mult)
                    dve.tensor_scalar(du[:, b, 2 * P:W2], c2("gt"), delta[:, 4, 8 + hd:9 + hd], None, ALU.mult).then_inc(*signal("du", l, hd))

                def ssd_y(j):
                    dve.wait_ge(*event("psum_full", "ssdY", l, j))
                    dve.scalar_tensor_tensor(y2(4 + j), xbc[:, j, :], p("d_skip", lw)[:, j:j + 1],
                                                 bank(("ssdY", l, j))[:, 0:T], ALU.mult, ALU.add).then_inc(*signal("ssd_skip", l, j))
                    dve.wait_ge(*event("ssd_skip", l, j))
                    dve.tensor_tensor(y2(4 + j), y2(4 + j), gate[:, 4 + j, :], ALU.mult).then_inc(*signal("ssd_gated", l, j))

                dve.wait_ge(*event("cb_masked", l, 1))
                ssd_du(0)
                ssd_du(1)
                for hd in range(8):
                    e = given("tmp", ("ssd_g", l, hd))
                    dve.wait_ge(*event("seg_exp", l, hd))
                    g = hd // 4
                    dve.scalar_tensor_tensor(e[:, 0:T], e[:, 0:T], delta[:, 1, hd:hd + 1], cbm[:, g, 0:T],
                                             ALU.mult, ALU.mult)
                    dve.scalar_tensor_tensor(e[:, T:W2], e[:, T:W2], delta[:, 1, 8 + hd:9 + hd], cbm[:, g, T:W2],
                                                 ALU.mult, ALU.mult).then_inc(*signal("ssd_g", l, hd))
                    if hd + 2 < 8:
                        ssd_du(hd + 2)
                    if hd % 2 == 0 and hd:
                        ssd_y(hd // 2 - 1)
                ssd_y(3)
                for g in range(2):
                    dve.wait_ge(*event("rs", ("ssd", g), l))
                    for k in range(2):
                        j = 2 * g + k
                        dve.scalar_tensor_tensor(y2(4 + j), y2(4 + j), p("ssd", lw)[:, j:j + 1],
                                                     given("rs", (("ssd", g), l))[:, 0:T], ALU.mult, ALU.mult).then_inc(*signal("gated", l, 4 + j))

                for hd in range(5):
                    if hd < 4:
                        e = take(dve, "work", ("ret_decay", l, hd), ("psum_full", "retY", l, hd))
                        dve.wait_ge(*event("psum_full", "retS", l, hd))
                        dve.tensor_tensor(e[:, 0:W2], bank(("retS", l, hd))[:, 0:W2],
                                              c2("decay")[:, W2 * hd:W2 * hd + W2], ALU.mult).then_inc(*signal("ret_decay", l, hd))
                    if hd:
                        dve.wait_ge(*event("psum_full", "retY", l, hd - 1))
                        dve.tensor_copy(y2(hd - 1), bank(("retY", l, hd - 1))[:, 0:T]).then_inc(*signal("ret_y", l, hd - 1))
                for hd in range(4):
                    dve.wait_ge(*event("psum_full", "retM", l, hd))
                    dve.scalar_tensor_tensor(y2(hd), bank(("retM", l, hd))[:, 0:T], -1.0 / P, y2(hd),
                                                 ALU.mult, ALU.add).then_inc(*signal("ret_centre", l, hd))
                for hd in range(4):
                    dve.wait_ge(*event("rs", ("ret", hd), l))
                    dve.wait_ge(*event("squared", ("ret", hd), l, 0))
                    then(dve.tensor_tensor(y2(hd), y2(hd), given("rs", (("ret", hd), l))[:, 0:T], ALU.mult))
                    dve.tensor_tensor(y2(hd), y2(hd), gate[:, hd, :], ALU.mult).then_inc(*signal("gated", l, hd))

                for hd in range(6):
                    if hd < 4:
                        z = take(dve, "work", ("sb_logit", l, hd), ("psum_full", "sbY", l, hd))[:, 0:W2]
                        dve.wait_ge(*event("psum_full", "sbS", l, hd))
                        dve.tensor_scalar(z, bank(("sbS", l, hd))[:, 0:W2], float(P) ** -0.5, None, ALU.mult).then_inc(*signal("sb_logit", l, hd))
                        dve.wait_ge(*event("sb_logit", l, hd))
                        s2 = take(dve, "work", ("sb_abs", l, hd), ("sb_log", l, hd))[:, 0:W2]
                        dve.scalar_tensor_tensor(s2, z, -1.0, z, ALU.mult, ALU.min).then_inc(*signal("sb_abs", l, hd))
                        s = given("sq", ("sb", l, hd))[:, 0:W2]
                        dve.wait_ge(*event("sb_log", l, hd))
                        then(dve.scalar_tensor_tensor(s, z, 0.0, s, ALU.max, ALU.add))
                        dve.tensor_tensor(s, s, c2("strict"), ALU.mult).then_inc(*signal("sb_softplus", l, hd))
                    if 0 < hd < 5:
                        v = hd - 1
                        z = given("work", ("sb_logit", l, v))[:, 0:W2]
                        dve.wait_ge(*event("psum_full", "sbT", l, v))
                        then(dve.scalar_tensor_tensor(z, bank(("sbT", l, v))[:, 0:W2], -1.0, z, ALU.mult, ALU.add))
                        dve.tensor_tensor(z, z, c2("neg"), ALU.add).then_inc(*signal("sb_tail", l, v))
                    if hd > 1:
                        v = hd - 2
                        dve.wait_ge(*event("psum_full", "sbY", l, v))
                        dve.tensor_tensor(y2(8 + v), bank(("sbY", l, v))[:, 0:T], gate[:, 8 + v, :], ALU.mult).then_inc(*signal("gated", l, 8 + v))

                def y_out(hd):
                    dve.wait_ge(*event("psum_full", ("memory", l), "Y", hd))
                    dve.tensor_tensor(y2(12 + hd), bank((("memory", l), "Y", hd))[:, 0:T], gate[:, 12 + hd, :],
                                          ALU.mult).then_inc(*signal("mem_gated", ("memory", l), hd))

                softmax(("memory", l), 8, T, False, y_out)

                for n in range(KT):
                    dve.wait_ge(*event("psum_full", "out2", l, n))
                    dve.tensor_copy(yo[:, n, :], bank(("out2", l, n))[:, 0:T]).then_inc(*signal("out_copied", l, n))
                dve.wait_ge(*event("rs", "n4", l))
                for k in range(KT):
                    then(dve.scalar_tensor_tensor(yo[:, k, :], yo[:, k, :], p("post", lw)[:, k:k + 1],
                                                  given("rs", ("n4", l))[:, 0:T], ALU.mult, ALU.mult))
                    dve.tensor_tensor(x2[:, k, :], x2[:, k, :], yo[:, k, :], ALU.add).then_inc(*signal("x_out", l, k))
    return seen


def lay_out(a):
    def cols(v):
        v = np.asarray(v, np.float32)
        return v.reshape(-1, P).T

    def pad(v):
        out = np.zeros((P, v.shape[0]), np.float32)
        out[:v.shape[1]] = v.T
        return out

    def feature_major(v):
        return np.ascontiguousarray(v.T.reshape(KT, P, -1).transpose(1, 0, 2))

    chunks, _ = weight_chunks()
    parts = []
    for entries, size in chunks:
        parts.append(np.concatenate([
            a[src][l, k0:k0 + P * nk][:, list(cc)].reshape(nk, P, len(cc)).transpose(1, 0, 2).reshape(P, -1)
            for _, src, l, k0, nk, cc in entries], axis=1).ravel())
    w = np.concatenate(parts)

    cvec = np.stack([a["c"][0], a["c_ctx"]])
    two = lambda v: np.concatenate([v, v], axis=1).T
    params = {
        "c": cvec.reshape(2, KT, P).transpose(2, 1, 0).reshape(P, -1),
        "b_ada": cols(a["b_ada"]), "g_attn": cols(a["g_attn"]), "g_mlp": cols(a["g_mlp"]),
        "g_qa": cols(a["g_qa"]), "g_kva": cols(a["g_kva"]), "g_mla_q": pad(a["g_mla_q"]),
        "g_mla_k": pad(a["g_mla_k"]), "g_na_q": two(a["g_na_q"]), "g_na_k": two(a["g_na_k"]),
        "pre": cols(a["pre_norm_g_2"]), "post": cols(a["post_norm_g_2"]), "mem": cols(a["mem_norm_g_2"]),
        "ssd": cols(a["ssd_norm_g_2"]),
        "conv_w": a["conv_w_2"].reshape(L, 4, 8, P).transpose(3, 0, 2, 1).reshape(P, -1),
        "conv_b": cols(a["conv_b_2"]), "d_skip": cols(np.repeat(a["d_skip_2"], 64, axis=1)),
        "dt_bias": np.broadcast_to(a["dt_bias_2"].reshape(1, -1), (P, 16)),
        "a_log": np.broadcast_to(a["a_log_2"].reshape(1, -1), (P, 16))}
    par = np.zeros((P, NPARAMS), np.float32)
    for name, v in params.items():
        par[:, PARAMS[name][0]:PARAMS[name][1]] = v

    rows = T // GRID
    q, k = np.arange(T)[:, None], np.arange(T)[None, :]
    qr, qc, kr, kc = q // GRID, q % GRID, k // GRID, k % GRID
    kh = min(KH, rows)
    r_start = np.clip(qr - kh // 2, 0, rows - kh)
    c_start = np.clip(qc - KW // 2, 0, GRID - KW)
    inside = (kr >= r_start) & (kr < r_start + kh) & (kc >= c_start) & (kc < c_start + KW)
    dr = np.clip(kr - qr + KH - 1, 0, 2 * KH - 2)
    dc = np.clip(kc - qc + KW - 1, 0, 2 * KW - 2)
    bias = np.where(inside, a["rpb"][:, :, dr, dc], np.float32(NEG))
    bias = np.ascontiguousarray(bias.reshape(L, NH, 2, P, T).transpose(0, 3, 2, 1, 4)).astype(np.float32)
    return {"w": w, "par": par, "bias": bias, "mem": feature_major(a["mem_2"][0]),
            "x": feature_major(np.concatenate([a["ctx"][0], a["x"][0]])), **constants()}


def constants():
    i = np.arange(P)
    con = np.zeros((P, NCONST), np.float32)
    put = lambda arr, table, name, v, r=slice(0, P): arr.__setitem__((r, slice(*table[name])), v)
    put(con, CONST, "ident", np.eye(P))
    put(con, CONST, "ones", 1.0)
    put(con, CONST, "pair", (i[:, None] // 64 == i[None, :] // 64))
    rot = np.zeros((ROPE, ROPE))
    for b in (0, 16):
        for m in range(8):
            rot[b + m + 8, b + m] = -1.0
            rot[b + m, b + m + 8] = 1.0
    put(con, CONST, "rot", rot, slice(NOPE, QK))
    put(con, CONST, "eps", EPS)
    put(con, CONST, "one", 1.0)
    t = np.arange(T)
    inv = (10000.0 ** (-np.arange(8, dtype=np.float32) / 8)).astype(np.float32)
    row = (t // GRID).astype(np.float32)[None, :] * inv[:, None]
    col = (t % GRID).astype(np.float32)[None, :] * inv[:, None]
    ang = np.concatenate([row, row, col, col])
    put(con, CONST, "cos", np.cos(ang), slice(NOPE, QK))
    put(con, CONST, "sin", np.sin(ang), slice(NOPE, QK))

    con2 = np.zeros((P, NCONST2), np.float32)
    causal_pair = lambda f: np.concatenate([f(i[:, None], t[None, :]), f(i[:, None] + P, t[None, P:])], axis=1)
    put(con2, CONST2, "gt", i[:, None] > i[None, :])
    put(con2, CONST2, "le", i[:, None] <= t[None, :])
    put(con2, CONST2, "ge", i[:, None] >= i[None, :])
    put(con2, CONST2, "causal", causal_pair(lambda s, l: s <= l))
    put(con2, CONST2, "strict", causal_pair(lambda s, l: s < l))
    put(con2, CONST2, "neg", causal_pair(lambda s, l: np.where(s < l, 0.0, NEG)))
    log_g = np.log(1.0 - 2.0 ** (-5.0 - np.arange(4)))
    put(con2, CONST2, "decay", np.concatenate([
        causal_pair(lambda s, l: np.where(s <= l, np.exp((l - s) * g), 0.0) * P ** -0.5) for g in log_g], axis=1))
    inv = (10000.0 ** (-np.arange(0, P, 2, dtype=np.float32) / P)).astype(np.float32)
    ang = t.astype(np.float32)[None, :] * inv[:, None]
    put(con2, CONST2, "cos", np.concatenate([np.cos(ang), np.cos(ang)]))
    put(con2, CONST2, "sin", np.concatenate([np.sin(ang), -np.sin(ang)]))
    return {"con": con, "con2": con2}


def kernel(**inputs):
    import concourse.bacc as bacc
    from concourse.bass_utils import run_bass_kernel_spmd

    arrays = lay_out({k: np.asarray(v) for k, v in inputs.items()})

    def build(numbers):
        nc = bacc.Bacc("TRN2", target_bir_lowering=False, num_devices=1)
        dram = {n: nc.dram_tensor(f"in_{n}", v.shape, F32, kind="ExternalInput").ap() for n, v in arrays.items()}
        dram["out"] = nc.dram_tensor("out_0", (P, KT, T), F32, kind="ExternalOutput").ap()
        return nc, program(nc, dram, numbers)

    _, numbers = build({})
    nc, again = build(numbers)
    assert again == numbers
    r = run_bass_kernel_spmd(nc, [{f"in_{n}": v for n, v in arrays.items()}], core_ids=[0])
    out = r.results[0]["out_0"]
    return np.ascontiguousarray(out.transpose(2, 1, 0).reshape(1, T, D))
```

```python
from contextlib import ExitStack

import numpy as np

import concourse.bass as bass
from concourse import mybir

F32 = mybir.dt.float32
ALU = mybir.AluOpType
ACT = mybir.ActivationFunctionType
AXX = mybir.AxisListType.X

P = 128
D, L, T, TC = 1024, 2, 256, 256
KT = D // P
TT = T + TC
QL, KVL, NH, NOPE, ROPE, VD = 768, 256, 8, 64, 32, 64
QK = NOPE + ROPE
ND = 64
FF = 4 * D
EPS = 1e-6
RING, SLOT = 5, 2048
BANKS = 8
W2 = 384
GRID, KW, KH = 64, 16, 8
NEG = -1e30
GATES = [4, 5, 6, 7, 0, 1, 2, 3] + list(range(8, 16))
ADA = 24
GT = 8
NG = FF // P // GT
SPLIT = ("g1", "mo", "no", "g2", "out", "ff1", "ff2")
F32R = mybir.dt.float32r
RAW = 3

C_CQ, C_CKV, C_KR, C_NA = 2 * D, 2 * D + QL, 2 * D + QL + KVL, 2 * D + QL + KVL + ROPE
(O_RQ, O_RK, O_RV, O_RG, O_XBC, O_Z, O_DT, O_SQ, O_SK, O_SV, O_SG, O_MQ, O_MG, _) = np.cumsum(
    [0, 512, 512, 512, 512, 1024, 512, 8, 512, 512, 512, 512, 512, 512]).tolist()


def weight_entries():
    out = []

    def add(key, src, l, k0, nk, cols):
        out.append((key, src, l, k0, nk, cols))

    for l in range(L):
        for j in range(ADA if l == 0 else 0):
            add(("ada", l, j), "w_ada", l, 0, KT, range(256 * j, 256 * j + 256))
        for i in range(6):
            add(("cq", l, i), "w_in", l, 0, KT, range(C_CQ + P * i, C_CQ + P * i + P))
        for i in range(2):
            add(("ckv", l, i), "w_in", l, 0, KT, range(C_CKV + P * i, C_CKV + P * i + P))
        add(("kr", l), "w_in", l, 0, KT, range(C_KR, C_KR + ROPE))
        for which, c0 in (("nq", C_NA), ("nk", C_NA + 512)):
            for i in range(4):
                add((which, l, i), "w_in", l, 0, KT, range(c0 + P * i, c0 + P * i + P))
        for h in range(NH):
            add(("uk", l, h), "w_ukv", l, 0, 2, range(P * h, P * h + NOPE))
        add(("uv", l), "w_ukv", l, 0, 2, [P * h + NOPE + e for h in range(NH) for e in range(VD)])
        for i in range(2):
            add(("nv", l, i), "w_in", l, 0, KT, range(C_NA + 1024 + 256 * i, C_NA + 1280 + 256 * i))
        for h in range(NH):
            add(("uq", l, h), "w_uq", l, 0, 6, range(QK * h, QK * h + QK))
        for j in range(ADA if l + 1 < L else 0):
            add(("ada", l + 1, j), "w_ada", l + 1, 0, KT, range(256 * j, 256 * j + 256))
        for n in range(KT):
            cols = range(P * n, P * n + P)
            add(("g1", l, n), "w_in", l, 0, KT, cols)
            add(("mo", l, n), "w_mla_o", l, 0, 4, cols)
            add(("no", l, n), "w_na_o", l, 0, 4, cols)
            add(("g2", l, n), "w_in", l, 0, KT, range(D + P * n, D + P * n + P))
        for n in range(KT):
            add(("out", l, n), "w_out", l, 0, KT, range(P * n, P * n + P))
        for g in range(NG):
            for n in range(GT * g, GT * g + GT):
                add(("ff1", l, n), "w_ff1", l, 0, KT, range(P * n, P * n + P))
            for n in range(KT):
                add(("ff2", l, g, n), "w_ff2", l, P * GT * g, GT, range(P * n, P * n + P))
    for l in range(L):
        for i in range(4):
            add(("memk", l, i), "w_mem_kv_2", l, 0, KT, range(P * i, P * i + P))
        for i in range(2):
            add(("memv", l, i), "w_mem_kv_2", l, 0, KT, range(512 + 256 * i, 768 + 256 * i))
        add(("dt", l), "w_in_2", l, 0, KT, range(O_DT, O_DT + 8))
        for which, c0, n in (("xbc", O_XBC, 8), ("rq", O_RQ, 4), ("rk", O_RK, 4), ("sq", O_SQ, 4),
                             ("sk", O_SK, 4), ("mq", O_MQ, 4)):
            for i in range(n):
                add((which, l, i), "w_in_2", l, 0, KT, range(c0 + P * i, c0 + P * i + P))
        for which, c0 in (("rv", O_RV), ("sv", O_SV)):
            for i in range(2):
                add((which, l, i), "w_in_2", l, 0, KT, range(c0 + 256 * i, c0 + 256 * i + 256))
        for i in GATES:
            c0 = (O_RG, O_Z, O_SG, O_MG)[i // 4] + P * (i % 4)
            add(("gate", l, i), "w_in_2", l, 0, KT, range(c0, c0 + P))
        for n in range(KT):
            add(("out2", l, n), "w_out_2", l, 0, 16, range(P * n, P * n + P))
    return out


def weight_chunks():
    chunks, place = [], {}
    for e in weight_entries():
        size = e[4] * len(e[5])
        split = e[0][0] in SPLIT
        if not chunks or chunks[-1][1] + size > SLOT or (chunks[-1][0][0][0][0] in SPLIT) != split:
            chunks.append([[], 0])
        place[e[0]] = (len(chunks) - 1, chunks[-1][1], e[4], len(e[5]))
        chunks[-1][0].append(e)
        chunks[-1][1] += size
    return chunks, place


def ring_slots(chunks):
    out, last, slot, pair, last_pair = [], {}, -1, 0, {}
    for i, (entries, _) in enumerate(chunks):
        split = entries[0][0][0] in SPLIT
        if split and not (i and out[i - 1][0]):
            pair, last_pair = 0, {}
        slot = (slot + 1) % (RAW if split else RING)
        out.append((split, slot, last.get(slot), pair if split else None, last_pair.get(pair)))
        last[slot] = i
        if split:
            last_pair[pair] = i
            pair = 1 - pair
    return out


def columns(sizes):
    at, out = 0, {}
    for name, n in sizes:
        out[name] = (at, at + n)
        at += n
    return out, at


PARAMS, NPARAMS = columns([
    ("c", 16), ("b_ada", 96), ("g_attn", 16), ("g_mlp", 16), ("g_qa", 12), ("g_kva", 4),
    ("g_mla_q", 2), ("g_mla_k", 2), ("g_na_q", 2), ("g_na_k", 2),
    ("pre", 16), ("post", 16), ("mem", 16), ("ssd", 8), ("conv_w", 64), ("conv_b", 16),
    ("d_skip", 8), ("dt_bias", 16), ("a_log", 16)])
CONST, NCONST = columns([("ident", P), ("ones", P), ("pair", P), ("rot", ROPE), ("eps", 1), ("one", 1),
                         ("cos", T), ("sin", T)])
CONST2, NCONST2 = columns([("gt", P), ("le", 2 * P), ("ge", P), ("causal", W2), ("strict", W2),
                           ("neg", W2), ("decay", 4 * W2), ("cos", T), ("sin", T)])


def program(nc, dram, numbers):
    chunks, place = weight_chunks()
    ctx = ExitStack()
    with ctx:
        def sb(name, shape):
            return ctx.enter_context(nc.sbuf_tensor(name, shape, F32))

        sems, count, seen, rings, turn, freed = {}, {}, {}, {}, {}, {}

        def sem(name):
            if name not in sems:
                sems[name] = ctx.enter_context(nc.semaphore(name))
                count[name] = 0
            return sems[name]

        def signal(name, *key, by=1):
            s = sem(name)
            count[name] += by
            assert (name, *key) not in seen, (name, *key)
            seen[(name, *key)] = count[name]
            return s, by

        def event(name, *key):
            assert not numbers or (name, *key) in numbers, (name, *key)
            return sem(name), numbers.get((name, *key), 1)

        def buffers(ring_name, items):
            rings[ring_name], turn[ring_name], freed[ring_name] = items, 0, [None] * len(items)

        def take(eng, ring_name, key, until):
            s = turn[ring_name] % len(rings[ring_name])
            turn[ring_name] += 1
            if freed[ring_name][s] is not None:
                eng.wait_ge(*event(*freed[ring_name][s]))
            freed[ring_name][s] = until
            seen[("slot", ring_name, key)] = s
            return rings[ring_name][s]

        def chunk_used(i):
            return numbers.get(("chunk_used", i), ("none",))

        def given(ring_name, key):
            return rings[ring_name][numbers.get(("slot", ring_name, key), 0)]

        def bank(key):
            return given("bank", key)

        buffers("bank", [ctx.enter_context(nc.psum_tensor(f"bank{i}", [P, 512], F32)) for i in range(BANKS)])

        ring_at = -(-nc.sbuf_base // 32) * 32
        ring = sb("ring", [P, RING, SLOT])
        h_at = ring_at + 4 * RING * SLOT
        h = sb("h", [P, KT, TT])
        wide_at = h_at + 4 * KT * TT
        wide = sb("wide", [P, 16384])
        assert nc.sbuf_base == wide_at + 4 * 16384
        x = sb("x", [P, KT, TT])
        sq_all = sb("sq", [P, 4, TT])
        rs_all = sb("rs", [P, 2, TT])
        tmp_all = sb("tmp", [P, 4, TT])
        par = sb("par", [P, NPARAMS])
        con = sb("con", [P, NCONST])
        mod_ctx = sb("mod_ctx", [P, L, 48])
        amp = sb("amp", [P, 2, KT, 2])
        silc = sb("silc", [P, 3, 16])
        gq = sb("gq", [P, 4])
        lowrank = sb("lowrank", [P, 4096])
        yT = sb("yT", [P, KT, TT])
        prob_all = sb("prob", [P, 3, TT])
        probT = sb("probT", [P, 2, 4, T])
        stat = sb("stat", [P, 4, 4])

        def part(name, shape, at):
            return nc.alloc_sbuf_tensor_at(name, shape, F32R, offset=at)

        w_parts = [part("w_parts0", [P, 2, SLOT], ring_at + 4 * RAW * SLOT), part("w_parts1", [P, 2, SLOT], h_at)]
        h_parts = part("h_parts", [P, 2, KT, TT], wide_at)
        b_parts = part("b_parts", [P, 2, KT, TT], wide_at + 4 * 8192)
        slots = ring_slots(chunks)

        buffers("sq", [sq_all[:, i, :] for i in range(4)])
        buffers("rs", [rs_all[:, i, :] for i in range(2)])
        buffers("tmp", [tmp_all[:, i, :] for i in range(4)])
        buffers("prob", [prob_all[:, i, :] for i in range(3)])
        krope = prob_all

        def p(name, l=None):
            a, b = PARAMS[name]
            n = (b - a) // L if l is not None else b - a
            return par[:, a + (l or 0) * n:a + (l or 0) * n + n]

        def mod(l, s):
            return mod_ctx[:, l, :] if s else p("b_ada", l)

        def c(name):
            return con[:, CONST[name][0]:CONST[name][1]]

        ident, ones, pair, eps, one = c("ident"), c("ones"), c("pair"), c("eps"), c("one")
        cq = lowrank[:, 0:3072].rearrange("p (k t) -> p k t", k=6)
        ckv = lowrank[:, 3072:4096].rearrange("p (k t) -> p k t", k=2)
        bias = lowrank[:, :].rearrange("p (q h k) -> p q h k", q=2, h=NH)
        yg = lowrank[:, :].rearrange("p (k t) -> p k t", k=KT)
        mq = wide[:, 0:4096].rearrange("p (h t) -> p h t", h=NH)
        mk = wide[:, 4096:8192].rearrange("p (h t) -> p h t", h=NH)
        nq = wide[:, 8192:10240].rearrange("p (h t) -> p h t", h=4)
        nk = wide[:, 10240:12288].rearrange("p (h t) -> p h t", h=4)
        mv = wide[:, 12288:14336].rearrange("p (t e) -> p t e", t=4)
        nv = wide[:, 14336:16384].rearrange("p (t e) -> p t e", t=4)
        heads1 = {"mq": mq, "mk": mk, "nq": nq, "nk": nk, "cq": cq, "ckv": ckv}

        x2 = x[:, :, TC:TT]
        h2 = h[:, :, 0:T]
        memn = h[:, :, T:TT]
        mem = wide[:, 0:2048].rearrange("p (k t) -> p k t", k=KT)
        conv_in = wide[:, 2048:2048 + 8 * T].rearrange("p (i t) -> p i t", i=8)
        at = 2048 + 8 * T
        xbc = wide[:, at:at + 2048].rearrange("p (i t) -> p i t", i=8)
        at += 2048
        heads2, vals2 = {}, {}
        for name in ("rq", "rk", "sq", "sk", "mq", "memk"):
            heads2[name] = wide[:, at:at + 1024].rearrange("p (h t) -> p h t", h=4)
            at += 1024
        for name in ("rv", "sv", "memv", "xs"):
            vals2[name] = wide[:, at:at + 1024].rearrange("p (t e) -> p t e", t=2)
            at += 1024
        assert at <= 16384
        gate = yT[:, :, :].rearrange("p k (a t) -> p (k a) t", a=2)
        yo = probT[:, :, :, :].rearrange("p a k t -> p (a k) t")
        du = prob_all[:, :, :].rearrange("p a t -> p (a t)")[:, 0:2 * W2].rearrange("p (a w) -> p a w", a=2)
        cbm = prob_all[:, :, :].rearrange("p a t -> p (a t)")[:, 2 * W2:4 * W2].rearrange("p (a w) -> p a w", a=2)
        rope_tmp = probT[:, 0, 0:2, :]
        work_all = probT[:, :, :, :].rearrange("p a k t -> p (a k t)")[:, 512:512 + 4 * W2]
        raw_all = probT[:, :, :, :].rearrange("p a k t -> p (a k t)")
        buffers("raw", [raw_all[:, TT * i:TT * i + TT] for i in range(4)])
        buffers("work", [work_all[:, W2 * i:W2 * i + W2] for i in range(4)])
        buffers("sb_abs", [cbm[:, i, :] for i in range(2)])
        con2 = lowrank[:, 0:NCONST2]
        delta = lowrank[:, NCONST2:NCONST2 + 96].rearrange("p (a w) -> p a w", a=6)

        def y2(k):
            return x[:, k, 0:T] if k < 8 else conv_in[:, k - 8, :]

        def c2(name):
            return con2[:, CONST2[name][0]:CONST2[name][1]]

        def q0(l):
            return 0 if l == 0 else TC

        def groups(l):
            mla = lambda hd: (hd, slice(0, QK))
            na = lambda hd: (hd // 2, slice(ND * (hd % 2), ND * (hd % 2) + ND))
            out = [("mla", mq, mk, mv, mla, TC, 4, 0)]
            if l == 0:
                out.append(("mlac", mq, mk, mv, mla, 0, 2, 0))
            out.append(("na", nq, nk, nv, na, TC, 4, 4))
            if l == 0:
                out.append(("nac", nq, nk, nv, na, 0, 2, 4))
            return out

        def modulation_step(l, gi, u):
            if l + 1 < L and u % 2 == 0 and NH * gi + u // 2 <= ADA:
                return NH * gi + u // 2
            return None

        block = ctx.enter_context(nc.Block())

        @block.tensor
        def _(pe):
            used = {"chunk": -1, "open": set()}

            def next_bank(*key, until):
                return take(pe, "bank", key, until)

            def weights(*key):
                i, off, nk, w = place[key]
                if i != used["chunk"]:
                    used["chunk"] = i
                    pe.wait_ge(*event(f"weights_in{slots[i][1]}", i))
                used["open"].add(i)
                return ring[:, slots[i][1], off:off + nk * w].rearrange("p (k w) -> p k w", k=nk)

            def split_linear(ps, key, parts, t0, ready):
                i, off, nk, w = place[key]
                if i != used["chunk"]:
                    used["chunk"] = i
                    pe.wait_ge(*event("w_lo", i))
                used["open"].add(i)
                w_hi, w_lo = (w_parts[slots[i][3]][:, a, off:off + nk * w].rearrange("p (k w) -> p k w", k=nk)
                              for a in range(2))
                for k in range(nk):
                    if ready:
                        pe.wait_ge(*event(*ready, k))
                    hi, lo = parts[:, 0, k, t0:TT], parts[:, 1, k, t0:TT]
                    pe.matmul(ps, w_hi[:, k, :], hi, start=k == 0, stop=False)
                    pe.matmul(ps, w_hi[:, k, :], lo, start=False, stop=False)
                    mm = pe.matmul(ps, w_lo[:, k, :], hi, start=False, stop=k == nk - 1)
                return mm

            def full(ins, *key):
                ins.then_inc(*signal("psum_full", *key))
                for i in used["open"]:
                    seen[("chunk_used", i)] = key
                used["open"] = set()

            def linear(out, w, src, ready=None, first=True, last=True):
                nk = w.shape[1]
                for k in range(nk):
                    if ready:
                        pe.wait_ge(*event(*ready, k))
                    mm = pe.matmul(out, w[:, k, :], src(k), start=first and k == 0, stop=last and k == nk - 1)
                return mm

            def sum_squares(name, l, n, w, stationary=ones):
                ps = next_bank("ss", name, l, until=("rs_log", name, l))
                for k in range(n):
                    pe.wait_ge(*event("squared", name, l, k))
                    mm = pe.matmul(ps[:, 0:w], stationary, given("sq", (name, l, k))[:, 0:w], start=k == 0, stop=k == n - 1)
                    if k < n - 1:
                        mm.then_inc(*signal("square_used", name, l, k))
                full(mm, "ss", name, l)

            def head_sum(name, i, l, w):
                if name in ("nq", "nk"):
                    return sum_squares((name, i), l, 1, w, pair)
                ps = next_bank("ss", (name, i), l, until=("rs_log", (name, i), l))
                s = given("sq", ((name, i), l, 0))
                pe.wait_ge(*event("squared", (name, i), l, 0))
                if name == "mk":
                    pe.matmul(ps[0:QK, 0:w], ones[0:NOPE, 0:QK], s[0:NOPE, 0:w], start=True, stop=False)
                    pe.wait_ge(*event("kr_squared", l))
                    mm = pe.matmul(ps[0:QK, 0:w], ones[NOPE:QK, 0:QK], krope[NOPE:QK, 1, TT - w:TT], start=False, stop=True)
                else:
                    mm = pe.matmul(ps[0:QK, 0:w], ones[0:QK, 0:QK], s[0:QK, 0:w], start=True, stop=True)
                full(mm, "ss", (name, i), l)

            def rotate(key, src, until):
                ps = next_bank(*key, until=until)
                mm = pe.matmul(ps[NOPE:QK, 0:T], c("rot")[NOPE:QK, :], src, start=True, stop=True)
                full(mm, *key)

            def value_tile(name, l, lw, src, i, t):
                w = weights(name, lw, i)
                ps = next_bank(name, l, i, t, until=("v_copied", name, l, i, t))
                for k in range(KT):
                    mm = pe.matmul(ps[:, 0:256], src(k)[:, P * t:P * t + P], w[:, k, :], start=k == 0, stop=k == KT - 1)
                full(mm, name, l, i, t)

            def values(name, l, lw, src):
                for i in range(2):
                    for t in range(2):
                        value_tile(name, l, lw, src, i, t)

            def softmax_attention(g, n, nk, score, value, until="y_copied", between=None):
                for u in range(n + 2):
                    if u < n:
                        ps = next_bank(g, "S", u, until=("exp", g, u))
                        full(score(ps, u), g, "S", u)
                        if between:
                            between(u)
                    if u >= 2:
                        pe.wait_ge(*event("probs", g, u - 2))
                        ps = next_bank(g, "T", u - 2, until=("probT", g, u - 2))
                        for k in range(nk):
                            mm = pe.transpose(ps[:, P * k:P * k + P], given("prob", (g, u - 2))[:, P * k:P * k + P], ident)
                        full(mm, g, "T", u - 2)
                    if u >= 4 and u % 2 == 0:
                        one_value(g, u // 2 - 2, value, until)
                one_value(g, n // 2 - 1, value, until)

            def one_value(g, hd, value, until):
                pe.wait_ge(*event("probT", g, 2 * hd + 1))
                ps = next_bank(g, "Y", hd, until=(until, g, hd))
                full(value(ps, hd), g, "Y", hd)

            def modulation(l, j):
                if j < ADA:
                    w = weights("ada", l, j)
                    ps = next_bank("ada", l, j, until=("ada_copied", l, j))
                    for k in range(KT):
                        mm = pe.matmul(ps[0:2, 0:256], silc[:, 2, 2 * k:2 * k + 2], w[:, k, :],
                                       start=k == 0, stop=k == KT - 1)
                    full(mm, "ada", l, j)
                if j:
                    ps = next_bank("adaT", l, j - 1, until=("mod", l, j - 1))
                    row = given("tmp", ("ada", l, j - 1))
                    pe.wait_ge(*event("ada_copied", l, j - 1))
                    for i in range(2):
                        mm = pe.transpose(ps[:, 2 * i:2 * i + 2], row[0:2, P * i:P * i + P], ident[0:2, 0:2])
                    full(mm, "adaT", l, j - 1)

            pe.wait_ge(*event("con_in"))

            for l in range(L):
                t0 = q0(l)
                cw = TT - t0
                if l == 0:
                    pe.wait_ge(*event("silu_c"))
                    for j in range(ADA + 1):
                        modulation(0, j)

                sum_squares("n1", l, KT, TT)
                for name, n, c0 in (("cq", 6, t0), ("ckv", 2, 0)):
                    for i in range(n):
                        ps = next_bank(name, l, i, until=("copied", name, l, i))
                        mm = linear(ps[:, 0:TT - c0], weights(name, l, i), lambda k: h[:, k, c0:TT], ("h", "n1", l))
                        full(mm, name, l, i)
                ps = next_bank("kr", l, 0, until=("copied", "kr", l, 0))
                full(linear(ps[NOPE:QK, :], weights("kr", l), lambda k: h[:, k, :]), "kr", l, 0)
                sum_squares("cq", l, 6, cw)
                sum_squares("ckv", l, 2, TT)
                for name, c0 in (("nq", t0), ("nk", 0)):
                    for i in range(5):
                        if i < 4:
                            ps = next_bank(name, l, i, until=("copied", name, l, i))
                            full(linear(ps[:, 0:TT - c0], weights(name, l, i), lambda k: h[:, k, c0:TT]), name, l, i)
                        if i:
                            head_sum(name, i - 1, l, TT - c0)
                pe.wait_ge(*event("kr_gain", l))
                rotate(("krot", l), krope[NOPE:QK, 2, TC:TT], ("krot_sin", l))
                for i in range(NH + 1):
                    if i < NH:
                        ps = next_bank("mk", l, i, until=("copied", "mk", l, i))
                        mm = linear(ps[0:NOPE, :], weights("uk", l, i), lambda k: ckv[:, k, :], ("normed", "ckv", l))
                        full(mm, "mk", l, i)
                    if i:
                        head_sum("mk", i - 1, l, TT)
                    if i < NH:
                        value_tile("nv", l, l, lambda k: h[:, k, :], i // 4, i % 4)
                for i in range(NH + 2):
                    if i < NH:
                        ps = next_bank("mq", l, i, until=("copied", "mq", l, i))
                        mm = linear(ps[0:QK, 0:cw], weights("uq", l, i), lambda k: cq[:, k, t0:TT], ("normed", "cq", l))
                        full(mm, "mq", l, i)
                    if i < 4:
                        w = weights("uv", l)
                        ps = next_bank("mv", l, 0, i, until=("v_copied", "mv", l, 0, i))
                        for k in range(2):
                            mm = pe.matmul(ps[:, :], ckv[:, k, P * i:P * i + P], w[:, k, :], start=k == 0, stop=k == 1)
                        full(mm, "mv", l, 0, i)
                    if 0 < i <= NH:
                        head_sum("mq", i - 1, l, cw)
                    if i > 1:
                        pe.wait_ge(*event("normed", ("mq", i - 2), l, 0))
                        rotate(("qrot", l, i - 2), mq[NOPE:QK, i - 2, TC:TT], ("q_sin", l, i - 2))

                for gi, (gname, qs, ks, vs, rows, qcol, nk, _) in enumerate(groups(l)):
                    def score(ps, u):
                        a, r = rows(u // 2)
                        q = qcol + P * (u % 2)
                        if gname[:3] == "mla":
                            pe.wait_ge(*event("roped", "mq", l, u // 2))
                            pe.wait_ge(*event("k_ready", l, u // 2))
                        else:
                            pe.wait_ge(*event("normed", ("nk", 3), l, 0))
                        return pe.matmul(ps[:, 0:P * nk], qs[r, a, q:q + P], ks[r, a, 0:P * nk], start=True, stop=True)

                    def value(ps, hd):
                        for i, t in [(0, t) for t in range(4)] + ([(1, t) for t in range(4)] if gname[0] == "n" else []):
                            pe.wait_ge(*event("v_copied", "mv" if gname[0] == "m" else "nv", l, i, t))
                        r = VD * (hd % 2)
                        for k in range(nk):
                            mm = pe.matmul(ps[r:r + VD, 0:T], vs[:, k, VD * hd:VD * hd + VD],
                                           probT[:, hd % 2, k, :], start=k == 0, stop=k == nk - 1)
                        return mm

                    def next_modulation(u):
                        if modulation_step(l, gi, u) is not None:
                            modulation(l + 1, modulation_step(l, gi, u))

                    softmax_attention((gname, l), 2 * NH, nk, score, value, between=next_modulation)

                for g in groups(l):
                    pe.wait_ge(*event("y_copied", (g[0], l), NH - 1))
                for n in range(KT):
                    for name, parts, by, ready in (("g1", h_parts, "gate_exp", ("h_lo", "h", l)),
                                                   ("mo", b_parts, "merged", ("b_lo", "y", l)),
                                                   ("no", b_parts[:, :, 4:8, :], "merged", ("b_lo", "y4", l)),
                                                   ("g2", h_parts, "gate_exp", None)):
                        ps = next_bank(name, l, n, until=(by, name, l, n))
                        full(split_linear(ps[:, 0:cw], (name, l, n), parts, t0, ready if n == 0 else None), name, l, n)
                for n in range(KT):
                    ps = next_bank("out", l, n, until=("x_attn", l, n))
                    full(split_linear(ps[:, 0:cw], ("out", l, n), b_parts, t0, ("b_lo", "yg", l) if n == 0 else None),
                         "out", l, n)
                sum_squares("n2", l, KT, cw)
                for g in range(NG):
                    for n in range(GT * g, GT * g + GT):
                        ps = next_bank("ff1", l, n, until=("relu", l, n))
                        full(split_linear(ps[:, 0:cw], ("ff1", l, n), h_parts, t0, ("h_lo", "n2", l) if n == 0 else None),
                             "ff1", l, n)
                    for n in range(KT):
                        ps = next_bank("ff2", l, g, n, until=("x_mlp", l, g, n))
                        full(split_linear(ps[:, 0:cw], ("ff2", l, g, n), b_parts, t0,
                                          ("b_lo", "ff", l, g) if n == 0 else None), "ff2", l, g, n)

            sum_squares("n3", L, KT, T)
            sum_squares("mem", 2, KT, T)
            pe.wait_ge(*event("con2_in"))
            for lw in range(L):
                l = L + lw

                def tiles(name, n, src, ready, by):
                    for i in range(n):
                        ps = next_bank(name, l, i, until=(by, name, l, i))
                        full(linear(ps[:, 0:T], weights(name, lw, i), lambda k: src[:, k, :], ready), name, l, i)

                def causal_scores(key, by, ks, qs):
                    ps = next_bank(*key, until=by)
                    pe.matmul(ps[:, 0:T], ks[:, 0:P], qs, start=True, stop=True)
                    full(pe.matmul(ps[:, T:W2], ks[:, P:T], qs[:, P:T], start=True, stop=True), *key)

                def causal_product(ps, v, g, rows=slice(0, P)):
                    pe.matmul(ps[rows, 0:T], v[:, 0, :], g[:, 0:T], start=True, stop=False)
                    return pe.matmul(ps[rows, P:T], v[:, 1, :], g[:, T:W2], start=False, stop=True)

                tiles("memk", 4, memn, ("memn", l), "copied2")
                if lw:
                    sum_squares("n3", l, KT, T)
                values("memv", l, lw, lambda k: memn[:, k, :])
                w = weights("dt", lw)
                ps = next_bank("dt", l, until=("dt_bias", l, 1))
                for t in range(2):
                    for k in range(KT):
                        pe.wait_ge(*event("h2", l, k))
                        mm = pe.matmul(ps[:, 8 * t:8 * t + 8], h2[:, k, P * t:P * t + P], w[:, k, :],
                                       start=k == 0, stop=k == KT - 1)
                full(mm, "dt", l)
                for name, n, by in (("xbc", 8, "copied"), ("rq", 4, "roped"), ("rk", 4, "roped"),
                                    ("sq", 4, "copied2"), ("sk", 4, "copied2"), ("mq", 4, "copied2")):
                    tiles(name, n, h2, ("h2", l), by)
                values("rv", l, lw, lambda k: h2[:, k, :])
                values("sv", l, lw, lambda k: h2[:, k, :])

                def gate_tile(n):
                    i = GATES[n]
                    ps = next_bank("gate", l, i, until=("gated_in", "gate", l, i))
                    full(linear(ps[:, 0:T], weights("gate", lw, i), lambda k: h2[:, k, :]), "gate", l, i)

                for t in range(2):
                    ps = next_bank("xsT", l, t, until=("v_copied", "xs", l, 0, t))
                    for i in range(4):
                        pe.wait_ge(*event("xbc", l, i))
                        mm = pe.transpose(ps[:, P * i:P * i + P], xbc[:, i, P * t:P * t + P], ident)
                    full(mm, "xsT", l, t)
                pe.wait_ge(*event("xbc", l, 7))
                for g in range(2):
                    causal_scores(("cb", l, g), ("cb_masked", l, g), xbc[:, 4 + g, :], xbc[:, 6 + g, :])

                def ssd_decay(hd):
                    pe.wait_ge(*event("du", l, hd))
                    ps = next_bank("seg", l, hd, until=("seg_exp", l, hd))
                    b = hd % 2
                    pe.matmul(ps[:, 0:T], du[:, b, 0:P], c2("le"), start=True, stop=False)
                    pe.matmul(ps[:, P:T], du[:, b, P:2 * P], c2("le")[:, 0:P], start=False, stop=True)
                    mm = pe.matmul(ps[:, T:W2], du[:, b, 2 * P:W2], c2("le")[:, 0:P], start=True, stop=True)
                    full(mm, "seg", l, hd)

                ssd_decay(0)
                for hd in range(8):
                    if hd < 7:
                        ssd_decay(hd + 1)
                    gate_tile(hd)
                    for t in range(2):
                        pe.wait_ge(*event("v_copied", "xs", l, 0, t))
                    pe.wait_ge(*event("ssd_g", l, hd))
                    if hd % 2 == 0:
                        ps_y = next_bank("ssdY", l, hd // 2, until=("ssd_skip", l, hd // 2))
                    mm = causal_product(ps_y, vals2["xs"][:, :, 64 * hd:64 * hd + 64], given("tmp", ("ssd_g", l, hd)),
                                        slice(64 * (hd % 2), 64 * (hd % 2) + 64))
                    full(mm, "ssdY", l, hd // 2) if hd % 2 else mm.then_inc(*signal("ssd_half", l, hd))
                for g in range(2):
                    sum_squares(("ssd", g), l, 2, T)

                def ret_scores(hd):
                    pe.wait_ge(*event("roped", "rk", l, hd))
                    causal_scores(("retS", l, hd), ("ret_decay", l, hd), heads2["rk"][:, hd, :], heads2["rq"][:, hd, :])

                ret_scores(0)
                for hd in range(4):
                    if hd < 3:
                        ret_scores(hd + 1)
                    gate_tile(8 + hd)
                    for t in range(2):
                        pe.wait_ge(*event("v_copied", "rv", l, hd // 2, t))
                    pe.wait_ge(*event("ret_decay", l, hd))
                    ps = next_bank("retY", l, hd, until=("ret_y", l, hd))
                    mm = causal_product(ps, vals2["rv"][:, :, P * hd:P * hd + P], given("work", ("ret_decay", l, hd)))
                    full(mm, "retY", l, hd)
                for hd in range(4):
                    pe.wait_ge(*event("ret_y", l, hd))
                    ps = next_bank("retM", l, hd, until=("ret_centre", l, hd))
                    full(pe.matmul(ps[:, 0:T], ones, y2(hd), start=True, stop=True), "retM", l, hd)
                for hd in range(4):
                    sum_squares(("ret", hd), l, 1, T)

                def sb_scores(hd):
                    pe.wait_ge(*event("copied2", "sk", l, hd))
                    causal_scores(("sbS", l, hd), ("sb_logit", l, hd), heads2["sk"][:, hd, :], heads2["sq"][:, hd, :])

                def sb_value(hd):
                    for t in range(2):
                        pe.wait_ge(*event("v_copied", "sv", l, hd // 2, t))
                    pe.wait_ge(*event("sb_w", l, hd))
                    ps = next_bank("sbY", l, hd, until=("gated", l, 8 + hd))
                    mm = causal_product(ps, vals2["sv"][:, :, P * hd:P * hd + P], given("work", ("sb_logit", l, hd)))
                    full(mm, "sbY", l, hd)

                sb_scores(0)
                for hd in range(6):
                    if hd < 3:
                        sb_scores(hd + 1)
                    if hd < 4:
                        gate_tile(12 + hd)
                    if 0 < hd < 5:
                        v = hd - 1
                        pe.wait_ge(*event("sb_softplus", l, v))
                        ps = next_bank("sbT", l, v, until=("sb_tail", l, v))
                        s = given("sq", ("sb", l, v))
                        pe.matmul(ps[:, 0:T], c2("ge"), s[:, 0:T], start=True, stop=False)
                        pe.matmul(ps[:, P:T], ones, s[:, T:W2], start=False, stop=True)
                        full(pe.matmul(ps[:, T:W2], c2("ge"), s[:, T:W2], start=True, stop=True), "sbT", l, v)
                    if hd > 1:
                        sb_value(hd - 2)

                def mem_score(ps, u):
                    hd, qt = divmod(u, 2)
                    pe.wait_ge(*event("copied2", "mq", l, hd))
                    pe.wait_ge(*event("copied2", "memk", l, hd))
                    return pe.matmul(ps[:, 0:T], heads2["mq"][:, hd, P * qt:P * qt + P], heads2["memk"][:, hd, :],
                                     start=True, stop=True)

                def mem_value(ps, hd):
                    for k in range(2):
                        pe.wait_ge(*event("v_copied", "memv", l, hd // 2, k))
                        mm = pe.matmul(ps[:, 0:T], vals2["memv"][:, k, P * hd:P * hd + P], probT[:, hd % 2, k, :],
                                       start=k == 0, stop=k == 1)
                    return mm

                softmax_attention(("memory", l), 8, 2, mem_score, mem_value, "mem_gated")

                for k in range(12):
                    pe.wait_ge(*event("gated", l, k))
                pe.wait_ge(*event("mem_gated", ("memory", l), 3))
                for n in range(KT):
                    ps = next_bank("out2", l, n, until=("out_copied", l, n))
                    full(linear(ps[:, 0:T], weights("out2", lw, n), y2), "out2", l, n)
                sum_squares("n4", l, KT, T)

        @block.sync
        def _(sp):
            sp.dma_start(par[:, :], dram["par"]).then_inc(*signal("par_in", by=16))
            sp.dma_start(con[:, :], dram["con"]).then_inc(*signal("con_in", by=16))
            sp.dma_start(x[:, :, :], dram["x"]).then_inc(*signal("x_in", by=16))
            at = 0
            for i, (_, size) in enumerate(chunks):
                split, slot, before, _, _ = slots[i]
                if before is not None and slots[before][0]:
                    sp.wait_ge(*event("w_lo", before))
                elif before is not None:
                    sp.wait_ge(*event("psum_full", *chunk_used(before)))
                if not split and i and slot >= RAW:
                    ended = [j for j in range(i) if slots[j][0]]
                    if ended:
                        sp.wait_ge(*event("psum_full", *chunk_used(ended[-1])))
                sp.dma_start(ring[:, slot, 0:size], dram["w"][at:at + P * size].rearrange("(p s) -> p s", p=P)).then_inc(*signal(f"weights_in{slot}", i, by=16))
                at += P * size
            sp.wait_ge(*event("x_out", 2 * L - 1, KT - 1))
            sp.dma_start(dram["out"], x2).then_inc(*signal("result_stored", by=16))
            sp.wait_ge(*event("result_stored"))

        @block.gpsimd
        def _(pool):
            for l in range(L):
                pool.wait_ge(*event("psum_full", "mq", l, NH - 1))
                pool.dma_start(bias[:, :, :, :], dram["bias"][l]).then_inc(*signal("bias_in", l, by=16))
            pool.wait_ge(*event("psum_full", "out", L - 1, KT - 1))
            pool.dma_start(con2, dram["con2"]).then_inc(*signal("con2_in", by=16))
            pool.wait_ge(*event("psum_full", "ff2", L - 1, NG - 1, KT - 1))
            pool.dma_start(mem, dram["mem"]).then_inc(*signal("mem_in", by=16))

        @block.scalar
        def _(act):
            def rms(name, l, n, rows, w, used):
                r = take(act, "rs", (name, l), used)[0:rows, 0:w]
                act.wait_ge(*event("psum_full", "ss", name, l))
                act.activation(r, bank(("ss", name, l))[0:rows, 0:w], ACT.Ln, bias=eps[0:rows, :], scale=1.0 / n).then_inc(*signal("rs_log", name, l))
                act.wait_ge(*event("rs_log", name, l))
                act.activation(r, r, ACT.Exp, scale=-0.5).then_inc(*signal("rs", name, l))

            def square(name, l, k, n, src, rows=slice(0, P)):
                until = ("square_used", name, l, k) if k < n - 1 else ("psum_full", "ss", name, l)
                s = take(act, "sq", (name, l, k), until)
                act.activation(s[rows, 0:src.shape[-1]], src, ACT.Square).then_inc(*signal("squared", name, l, k))

            def copy_values(name, l, i, t, dst, src_key):
                act.wait_ge(*event("psum_full", *src_key))
                act.activation(dst, bank(src_key)[:, 0:dst.shape[-1]], ACT.Copy).then_inc(*signal("v_copied", name, l, i, t))

            def modulation(l, j):
                if j < ADA:
                    row = take(act, "tmp", ("ada", l, j), ("psum_full", "adaT", l, j))
                    act.wait_ge(*event("psum_full", "ada", l, j))
                    act.activation(row[0:2, 0:256], bank(("ada", l, j))[0:2, 0:256], ACT.Copy).then_inc(*signal("ada_copied", l, j))

            def softmax(g, n, w, between=None):
                for u in range(n + 2):
                    if u < n:
                        e = take(act, "prob", (g, u), ("psum_full", g, "T", u))
                        act.wait_ge(*event("neg_max", g, u))
                        act.activation(e[:, 0:w], bank((g, "S", u))[:, 0:w], ACT.Exp, bias=stat[:, u % 4, 0:1],
                                           accum_out=stat[:, u % 4, 1:2]).then_inc(*signal("exp", g, u))
                        if between:
                            between(u)
                    if u >= 2:
                        v = u - 2
                        act.wait_ge(*event("psum_full", g, "T", v))
                        if v >= 4:
                            act.wait_ge(*event("psum_full", g, "Y", v // 2 - 2))
                        act.activation(probT[:, (v // 2) % 2, 0:w // P, P * (v % 2):P * (v % 2) + P],
                                           bank((g, "T", v))[:, 0:w].rearrange("p (k q) -> p k q", q=P), ACT.Copy).then_inc(*signal("probT", g, v))

            split_next = {"at": 0}

            def split_weights(key, l):
                for i in range(split_next["at"], place[key][0] + 2):
                    split, slot, _, pair, before = slots[i]
                    split_next["at"] = i + 1
                    if not split:
                        continue
                    size = chunks[i][1]
                    act.wait_ge(*event(f"weights_in{slot}", i))
                    if before is not None:
                        act.wait_ge(*event("psum_full", *chunk_used(before)))
                    elif pair == 0:
                        for s in range(RAW, RING):
                            act.wait_ge(*event("psum_full", *chunk_used(max(
                                j for j in range(i) if not slots[j][0] and slots[j][1] == s))))
                    else:
                        act.wait_ge(*event("h_lo", "h", l, KT - 1))
                    act.activation(w_parts[pair][:, 0, 0:size], ring[:, slot, 0:size], ACT.Copy).then_inc(*signal("w_hi", i))

            act.preload_act_table_set("natural_log_exp_and_others")
            act.wait_ge(*event("par_in"))
            act.activation(silc[:, 0, :], p("c"), ACT.Exp, scale=-1.0).then_inc(*signal("c_exp"))
            act.wait_ge(*event("con_in"))
            act.wait_ge(*event("x_in"))

            for l in range(L):
                t0 = q0(l)
                cw = TT - t0

                def norm(name, c0, base):
                    for k in range(KT if name == "n1" else 0):
                        if l:
                            act.wait_ge(*event("x_mlp", l - 1, NG - 1, k))
                        square(name, l, k, KT, x[:, k, c0:TT])
                    rms(name, l, D, P, TT - c0, ("scaled", name, l, KT - 1))
                    if name == "n2":
                        for k in range(KT):
                            act.wait_ge(*event("scaled", name, l, k))
                            if k == 0:
                                act.wait_ge(*event("psum_full", "g2", l, KT - 1))
                            r = given("raw", ("n2", l, k))
                            for s in ((1, 0) if c0 == 0 else (0,)):
                                cols = slice((1 - s) * TC, (1 - s) * TC + TC)
                                ins = act.activation(h_parts[:, 0, k, cols], r[:, cols], ACT.Identity,
                                                     bias=mod(l, s)[:, base + k:base + k + 1])
                            ins.then_inc(*signal("h_hi", name, l, k))
                        return
                    for k in range(KT):
                        act.wait_ge(*event("scaled", name, l, k))
                        for s in ((1, 0) if c0 == 0 else (0,)):
                            cols = slice((1 - s) * TC, (1 - s) * TC + TC)
                            ins = act.activation(h[:, k, cols], h[:, k, cols], ACT.Identity,
                                                 bias=mod(l, s)[:, base + k:base + k + 1])
                        ins.then_inc(*signal("h", name, l, k))

                if l == 0:
                    for j in range(ADA):
                        modulation(0, j)
                norm("n1", 0, 0)

                for name, n, c0 in (("cq", 6, t0), ("ckv", 2, 0)):
                    for i in range(n):
                        act.wait_ge(*event("copied", name, l, i))
                        square(name, l, i, n, heads1[name][:, i, c0:TT])
                act.wait_ge(*event("copied", "kr", l, 0))
                act.activation(krope[NOPE:QK, 1, :], krope[NOPE:QK, 0, :], ACT.Square).then_inc(*signal("kr_squared", l))
                rms("cq", l, QL, P, cw, ("normed", "cq", l, 5))
                rms("ckv", l, KVL, P, TT, ("normed", "ckv", l, 1))
                for name, c0 in (("nq", t0), ("nk", 0)):
                    for i in range(5):
                        if i < 4:
                            act.wait_ge(*event("copied", name, l, i))
                            square((name, i), l, 0, 1, heads1[name][:, i, c0:TT])
                        if i:
                            rms((name, i - 1), l, ND, P, TT - c0, ("normed", (name, i - 1), l, 0))
                for i in range(NH + 1):
                    if i < NH:
                        act.wait_ge(*event("copied", "mk", l, i))
                        square(("mk", i), l, 0, 1, mk[0:NOPE, i, :], slice(0, NOPE))
                    if i:
                        rms(("mk", i - 1), l, QK, QK, TT, ("k_ready", l, i - 1))
                    if i < NH:
                        j, t = divmod(i, 4)
                        copy_values("nv", l, j, t, nv[:, t, 256 * j:256 * j + 256], ("nv", l, j, t))
                for i in range(NH + 1):
                    if i < NH:
                        act.wait_ge(*event("copied", "mq", l, i))
                        square(("mq", i), l, 0, 1, mq[0:QK, i, t0:TT], slice(0, QK))
                    if i < 4:
                        copy_values("mv", l, 0, i, mv[:, i, :], ("mv", l, 0, i))
                    if i:
                        rms(("mq", i - 1), l, QK, QK, cw, ("normed", ("mq", i - 1), l, 0))

                for gi, (gname, _, _, _, _, _, nk, _) in enumerate(groups(l)):
                    if gname == "na":
                        act.wait_ge(*event("psum_full", ("mla" if l else "mlac", l), "Y", NH - 1))
                        act.wait_ge(*event("psum_full", "nv", l, 1, 3))
                        for k in range(KT):
                            act.activation(h_parts[:, 0, k, t0:TT], h[:, k, t0:TT], ACT.Copy).then_inc(*signal("h_hi", "h", l, k))
                    def next_modulation(u):
                        if modulation_step(l, gi, u) is not None:
                            modulation(l + 1, modulation_step(l, gi, u))

                    softmax((gname, l), 2 * NH, P * nk, next_modulation)
                split_weights(("g1", l, 0), l)
                last = ("na" if l else "nac", l)
                for k in range(KT):
                    act.wait_ge(*event("y_copied", last, NH - 1))
                    act.activation(b_parts[:, 0, k, t0:TT], yT[:, k, t0:TT], ACT.Copy).then_inc(*signal("b_hi", "y", l, k))

                for n in range(KT):
                    split_weights(("g1", l, n), l)
                    for name, other in (("g1", "mo"), ("g2", "no")):
                        split_weights((name, l, n), l)
                        e = take(act, "tmp", (name, l, n), ("yg", l, n))
                        act.wait_ge(*event("psum_full", name, l, n))
                        act.activation(e[:, 0:cw], bank((name, l, n))[:, 0:cw], ACT.Exp, scale=-1.0).then_inc(*signal("gate_exp", name, l, n))
                for k in range(KT):
                    act.wait_ge(*event("yg", l, k))
                    act.wait_ge(*event("psum_full", "no", l, KT - 1))
                    act.activation(b_parts[:, 0, k, t0:TT], yg[:, k, t0:TT], ACT.Copy).then_inc(*signal("b_hi", "yg", l, k))
                for n in range(KT):
                    split_weights(("out", l, n), l)
                    act.wait_ge(*event("x_attn", l, n))
                    square("n2", l, n, KT, x[:, n, t0:TT])
                norm("n2", t0, 24)
                for g in range(NG):
                    for n in range(GT * g, GT * g + GT):
                        split_weights(("ff1", l, n), l)
                        r = given("raw", ("ff", l, n))[:, t0:TT]
                        act.wait_ge(*event("relu", l, n))
                        act.activation(r, r, ACT.Square).then_inc(*signal("relu_squared", l, n))
                        act.wait_ge(*event("relu_squared", l, n))
                        act.activation(b_parts[:, 0, n % GT, t0:TT], r, ACT.Copy).then_inc(*signal("b_hi", "ff", l, g, n % GT))
                    for n in range(KT):
                        split_weights(("ff2", l, g, n), l)

            def norm3(l):
                for k in range(KT):
                    if l > L:
                        act.wait_ge(*event("x_out", l - 1, k))
                    else:
                        act.wait_ge(*event("x_mlp", L - 1, NG - 1, k))
                    square("n3", l, k, KT, x2[:, k, :])
                rms("n3", l, D, P, T, ("h2", l, KT - 1))

            norm3(L)
            act.wait_ge(*event("mem_in"))
            for k in range(KT):
                square("mem", 2, k, KT, mem[:, k, :])
            rms("mem", 2, D, P, T, ("mem_normed", KT - 1))
            for lw in range(L):
                l = L + lw
                for i in range(4):
                    act.wait_ge(*event("psum_full", "memk", l, i))
                    act.activation(heads2["memk"][:, i, :], bank(("memk", l, i))[:, 0:T], ACT.Copy).then_inc(*signal("copied2", "memk", l, i))
                if lw:
                    norm3(l)
                for i in range(2):
                    for t in range(2):
                        copy_values("memv", l, i, t, vals2["memv"][:, t, 256 * i:256 * i + 256], ("memv", l, i, t))

                act.wait_ge(*event("dt_abs", l))
                act.activation(delta[:, 2, :], delta[:, 1, :], ACT.Exp).then_inc(*signal("dt_exp", l))
                act.wait_ge(*event("dt_exp", l))
                act.activation(delta[:, 3, :], delta[:, 2, :], ACT.Ln, bias=one).then_inc(*signal("dt_log", l))
                act.activation(delta[:, 5, 0:8], p("a_log", lw), ACT.Exp).then_inc(*signal("a_exp", l))
                for i in range(8):
                    e = take(act, "tmp", ("conv", l, i), ("xbc", l, i))
                    act.wait_ge(*event("conv", l, i))
                    act.activation(e[:, 0:T], xbc[:, i, :], ACT.Exp, scale=-1.0).then_inc(*signal("conv_exp", l, i))
                for name in ("sq", "sk", "mq"):
                    for i in range(4):
                        act.wait_ge(*event("psum_full", name, l, i))
                        act.activation(heads2[name][:, i, :], bank((name, l, i))[:, 0:T], ACT.Copy,
                                           scale=float(P) ** -0.5 if name == "mq" else 1.0).then_inc(*signal("copied2", name, l, i))
                for name in ("rv", "sv"):
                    for i in range(2):
                        for t in range(2):
                            copy_values(name, l, i, t, vals2[name][:, t, 256 * i:256 * i + 256], (name, l, i, t))

                def gate_exp(n):
                    i = GATES[n]
                    e = take(act, "tmp", ("gate", l, i), ("gated_in", "gate", l, i))
                    act.wait_ge(*event("psum_full", "gate", l, i))
                    act.activation(e[:, 0:T], bank(("gate", l, i))[:, 0:T], ACT.Exp, scale=-1.0).then_inc(*signal("gate_exp2", l, i))
                for t in range(2):
                    copy_values("xs", l, 0, t, vals2["xs"][:, t, :], ("xsT", l, t))
                for hd in range(8):
                    e = take(act, "tmp", ("ssd_g", l, hd),
                                 ("psum_full", "ssdY", l, hd // 2) if hd % 2 else ("ssd_half", l, hd))
                    act.wait_ge(*event("psum_full", "seg", l, hd))
                    act.activation(e[:, 0:W2], bank(("seg", l, hd))[:, 0:W2], ACT.Exp).then_inc(*signal("seg_exp", l, hd))
                    gate_exp(hd)
                for g in range(2):
                    for k in range(2):
                        act.wait_ge(*event("ssd_gated", l, 2 * g + k))
                        square(("ssd", g), l, k, 2, y2(4 + 2 * g + k))
                    rms(("ssd", g), l, 256, P, T, ("gated", l, 5 + 2 * g))
                for hd in range(4):
                    gate_exp(8 + hd)
                for hd in range(4):
                    act.wait_ge(*event("ret_centre", l, hd))
                    square(("ret", hd), l, 0, 1, y2(hd))
                for hd in range(4):
                    rms(("ret", hd), l, P, P, T, ("gated", l, hd))
                for hd in range(6):
                    if hd < 4:
                        s = take(act, "sq", ("sb", l, hd), ("psum_full", "sbT", l, hd))
                        s2 = given("sb_abs", (l, hd))
                        act.wait_ge(*event("sb_abs", l, hd))
                        act.activation(s2[:, 0:W2], s2[:, 0:W2], ACT.Exp).then_inc(*signal("sb_exp", l, hd))
                        act.wait_ge(*event("sb_exp", l, hd))
                        act.activation(s[:, 0:W2], s2[:, 0:W2], ACT.Ln, bias=one).then_inc(*signal("sb_log", l, hd))
                        gate_exp(12 + hd)
                    if hd > 1:
                        z = given("work", ("sb_logit", l, hd - 2))[:, 0:W2]
                        act.wait_ge(*event("sb_tail", l, hd - 2))
                        act.activation(z, z, ACT.Exp).then_inc(*signal("sb_w", l, hd - 2))
                softmax(("memory", l), 8, T)
                for k in range(KT):
                    act.wait_ge(*event("out_copied", l, k))
                    square("n4", l, k, KT, yo[:, k, :])
                rms("n4", l, D, P, T, ("x_out", l, KT - 1))

        @block.vector
        def _(dve):
            steps = [0]

            def then(ins):
                steps[0] += 1
                ins.then_inc(*signal("vector_step", steps[0]))
                dve.wait_ge(*event("vector_step", steps[0]))

            def copy(name, l, i, dst, rows=slice(0, P)):
                dve.wait_ge(*event("psum_full", name, l, i))
                dve.tensor_copy(dst, bank((name, l, i))[rows, 0:dst.shape[-1]]).then_inc(*signal("copied", name, l, i))

            def scale_norm(name, l, k, dst, gain, rows, w, slot, last=True):
                dve.wait_ge(*event("rs", *slot))
                dve.scalar_tensor_tensor(dst, dst, gain, given("rs", slot)[rows, 0:w], ALU.mult, ALU.mult).then_inc(*signal("normed", name, l, k))

            def sigmoid(e):
                then(dve.tensor_scalar(e, e, 1.0, None, ALU.add))
                then(dve.reciprocal(e, e))

            def softmax(g, n, w, biased, y_out, between=None):
                for u in range(n + 5):
                    if u < n:
                        s = bank((g, "S", u))
                        dve.wait_ge(*event("psum_full", g, "S", u))
                        if biased:
                            hd, qt = divmod(u, 2)
                            then(dve.tensor_tensor(s[:, TC:TT], s[:, TC:TT], bias[:, qt, hd, :], ALU.add))
                        dve.tensor_reduce(stat[:, u % 4, 0:1], s[:, 0:w], AXX, ALU.max, negate=True).then_inc(*signal("neg_max", g, u))
                    if 1 <= u <= n:
                        v = u - 1
                        dve.wait_ge(*event("exp", g, v))
                        then(dve.reciprocal(stat[:, v % 4, 2:3], stat[:, v % 4, 1:2]))
                        e = given("prob", (g, v))[:, 0:w]
                        dve.tensor_scalar(e, e, stat[:, v % 4, 2:3], None, ALU.mult).then_inc(*signal("probs", g, v))
                    if u >= 5 and u % 2 == 1 and (u - 5) // 2 < n // 2:
                        y_out((u - 5) // 2)
                    if between and u < n:
                        between(u)

            split_next = {"at": 0}

            def split_weights(key):
                for i in range(split_next["at"], place[key][0] + 2):
                    split, slot, _, pair, _ = slots[i]
                    split_next["at"] = i + 1
                    if not split:
                        continue
                    size = chunks[i][1]
                    dve.wait_ge(*event("w_hi", i))
                    dve.tensor_tensor(w_parts[pair][:, 1, 0:size], ring[:, slot, 0:size],
                                      w_parts[pair][:, 0, 0:size].bitcast(F32), ALU.subtract).then_inc(*signal("w_lo", i))

            def low_part(parts, k, src, cols, name, *key):
                dve.wait_ge(*event(f"{name}_hi", *key, k))
                dve.tensor_tensor(parts[:, 1, k, cols], src, parts[:, 0, k, cols].bitcast(F32),
                                  ALU.subtract).then_inc(*signal(f"{name}_lo", *key, k))

            dve.wait_ge(*event("par_in"))
            dve.wait_ge(*event("c_exp"))
            then(dve.tensor_scalar(silc[:, 1, :], silc[:, 0, :], 1.0, None, ALU.add))
            then(dve.reciprocal(silc[:, 0, :], silc[:, 1, :]))
            dve.tensor_tensor(silc[:, 2, :], silc[:, 0, :], p("c"), ALU.mult).then_inc(*signal("silu_c"))
            for i, (name, n) in enumerate((("g_mla_q", QK), ("g_na_q", ND))):
                then(dve.tensor_scalar(gq[:, 2 * i:2 * i + 2], p(name), float(n) ** -0.5, None, ALU.mult))

            def modulation(l, j):
                j -= 1
                if j < 0:
                    return
                a = bank(("adaT", l, j))[:, 0:4].rearrange("p (n s) -> p n s", s=2)
                dve.wait_ge(*event("psum_full", "adaT", l, j))
                for s in (1, 0):
                    ins = dve.tensor_tensor(mod(l, s)[:, 2 * j:2 * j + 2], a[:, :, s], p("b_ada", l)[:, 2 * j:2 * j + 2],
                                            ALU.add)
                ins.then_inc(*signal("mod", l, j))

            for l in range(L):
                t0 = q0(l)
                cw = TT - t0

                def norm(name, c0, which):
                    dve.wait_ge(*event("rs", name, l))
                    r = given("rs", (name, l))
                    for k in range(KT):
                        for s in ((1, 0) if c0 == 0 else (0,)):
                            cols = slice((1 - s) * TC, (1 - s) * TC + TC)
                            ins = dve.scalar_tensor_tensor(h[:, k, cols], x[:, k, cols], amp[:, which, k, s:s + 1],
                                                           r[:, cols.start - c0:cols.stop - c0], ALU.mult, ALU.mult)
                        ins.then_inc(*signal("scaled", name, l, k))

                if l == 0:
                    for j in range(ADA + 1):
                        modulation(0, j)
                dve.wait_ge(*event("mod", l, ADA - 1))
                for which, g in ((0, "g_attn"), (1, "g_mlp")):
                    for s in range(2):
                        at = 8 + 24 * which
                        then(dve.scalar_tensor_tensor(amp[:, which, :, s], mod(l, s)[:, at:at + 8], 1.0, p(g, l),
                                                      ALU.add, ALU.mult))
                norm("n1", 0, 0)
                for name, n, c0 in (("cq", 6, t0), ("ckv", 2, 0)):
                    for i in range(n):
                        copy(name, l, i, heads1[name][:, i, c0:TT])
                dve.wait_ge(*event("psum_full", "kr", l, 0))
                dve.tensor_copy(krope[NOPE:QK, 0, :], bank(("kr", l, 0))[NOPE:QK, :]).then_inc(*signal("copied", "kr", l, 0))
                dve.wait_ge(*event("copied", "kr", l, 0))
                dve.tensor_scalar(krope[NOPE:QK, 2, :], krope[NOPE:QK, 0, :], p("g_mla_k", l)[NOPE:QK, :], None,
                                      ALU.mult).then_inc(*signal("kr_gain", l))
                for name, n, c0, g in (("cq", 6, t0, "g_qa"), ("ckv", 2, 0, "g_kva")):
                    for i in range(n):
                        scale_norm(name, l, i, heads1[name][:, i, c0:TT], p(g, l)[:, i:i + 1], slice(0, P), TT - c0, (name, l))
                for name, c0 in (("nq", t0), ("nk", 0)):
                    gain = gq[:, 2 + l:3 + l] if name == "nq" else p("g_na_k", l)
                    for i in range(5):
                        if i < 4:
                            copy(name, l, i, heads1[name][:, i, c0:TT])
                        if i:
                            dve.wait_ge(*event("squared", (name, i - 1), l, 0))
                            scale_norm((name, i - 1), l, 0, heads1[name][:, i - 1, c0:TT], gain, slice(0, P), TT - c0,
                                       ((name, i - 1), l))
                kr = krope[NOPE:QK, 2, TC:TT]
                e = krope[NOPE:QK, 0, 0:T]
                dve.wait_ge(*event("psum_full", "krot", l))
                dve.wait_ge(*event("kr_squared", l))
                dve.tensor_tensor(e, bank(("krot", l))[NOPE:QK, 0:T], c("sin")[NOPE:QK, :], ALU.mult).then_inc(*signal("krot_sin", l))
                then(dve.tensor_tensor(kr, kr, c("cos")[NOPE:QK, :], ALU.mult))
                dve.wait_ge(*event("krot_sin", l))
                then(dve.tensor_tensor(kr, kr, e, ALU.add))
                for i in range(NH + 1):
                    if i < NH:
                        copy("mk", l, i, mk[0:NOPE, i, :], slice(0, NOPE))
                    if i:
                        v = i - 1
                        dve.wait_ge(*event("rs", ("mk", v), l))
                        r = given("rs", (("mk", v), l))
                        dve.scalar_tensor_tensor(mk[0:NOPE, v, :], mk[0:NOPE, v, :], p("g_mla_k", l)[0:NOPE, :],
                                                 r[0:NOPE, :], ALU.mult, ALU.mult)
                        dve.tensor_tensor(mk[NOPE:QK, v, :], krope[NOPE:QK, 2, :], r[NOPE:QK, :], ALU.mult).then_inc(*signal("k_ready", l, v))
                for i in range(NH + 2):
                    if i < NH:
                        copy("mq", l, i, mq[0:QK, i, t0:TT], slice(0, QK))
                    if 0 < i <= NH:
                        v = i - 1
                        scale_norm(("mq", v), l, 0, mq[0:QK, v, t0:TT], gq[0:QK, l:l + 1], slice(0, QK), cw, (("mq", v), l))
                    if i > 1:
                        v = i - 2
                        e = krope[NOPE:QK, 0, T * (v % 2):T * (v % 2) + T]
                        q = mq[NOPE:QK, v, TC:TT]
                        dve.wait_ge(*event("psum_full", "qrot", l, v))
                        dve.tensor_tensor(e, bank(("qrot", l, v))[NOPE:QK, 0:T], c("sin")[NOPE:QK, :], ALU.mult).then_inc(*signal("q_sin", l, v))
                        then(dve.tensor_tensor(q, q, c("cos")[NOPE:QK, :], ALU.mult))
                        dve.wait_ge(*event("q_sin", l, v))
                        dve.tensor_tensor(q, q, e, ALU.add).then_inc(*signal("roped", "mq", l, v))

                for gi, (gname, _, _, _, _, qcol, nk, y0) in enumerate(groups(l)):
                    def y_out(hd):
                        r = slice(VD * (hd % 2), VD * (hd % 2) + VD)
                        dve.wait_ge(*event("psum_full", (gname, l), "Y", hd))
                        dve.tensor_copy(yT[r, y0 + hd // 2, qcol:qcol + T], bank(((gname, l), "Y", hd))[r, 0:T]).then_inc(*signal("y_copied", (gname, l), hd))

                    if gname == "na":
                        for k in range(KT):
                            low_part(h_parts, k, h[:, k, t0:TT], slice(t0, TT), "h", "h", l)
                        dve.wait_ge(*event("bias_in", l))
                    def next_modulation(u):
                        if modulation_step(l, gi, u) is not None:
                            modulation(l + 1, modulation_step(l, gi, u))

                    softmax((gname, l), 2 * NH, P * nk, gname == "na", y_out, next_modulation)

                split_weights(("g1", l, 0))
                for k in range(KT):
                    dve.wait_ge(*event("b_hi", "y", l, k))
                    ins = dve.tensor_tensor(b_parts[:, 1, k, t0:TT], yT[:, k, t0:TT],
                                            b_parts[:, 0, k, t0:TT].bitcast(F32), ALU.subtract)
                    ins.then_inc(*(signal("b_lo", "y", l, k) if k < 4 else signal("b_lo", "y4", l, k - 4)))
                for n in range(KT):
                    es = []
                    for name, other in (("g1", "mo"), ("g2", "no")):
                        split_weights((name, l, n))
                        e = given("tmp", (name, l, n))[:, 0:cw]
                        dve.wait_ge(*event("gate_exp", name, l, n))
                        sigmoid(e)
                        dve.wait_ge(*event("psum_full", other, l, n))
                        dve.tensor_tensor(e, e, bank((other, l, n))[:, 0:cw], ALU.mult).then_inc(*signal("merged", other, l, n))
                        es.append(e)
                    dve.wait_ge(*event("merged", "no", l, n))
                    dve.tensor_tensor(yg[:, n, t0:TT], es[0], es[1], ALU.add).then_inc(*signal("yg", l, n))
                for k in range(KT):
                    low_part(b_parts, k, yg[:, k, t0:TT], slice(t0, TT), "b", "yg", l)

                def residual(n, base, done, *key):
                    dve.wait_ge(*event("psum_full", *key))
                    for s in ((1, 0) if t0 == 0 else (0,)):
                        cols = slice((1 - s) * TC, (1 - s) * TC + TC)
                        ins = dve.scalar_tensor_tensor(
                            x[:, n, cols], bank(key)[:, cols.start - t0:cols.stop - t0],
                            mod(l, s)[:, base + n:base + n + 1], x[:, n, cols], ALU.mult, ALU.add)
                    ins.then_inc(*signal(done, *key[1:]))

                for n in range(KT):
                    split_weights(("out", l, n))
                    residual(n, 16, "x_attn", "out", l, n)
                dve.wait_ge(*event("rs", "n2", l))
                for k in range(KT + 1):
                    if k < KT:
                        r = take(dve, "raw", ("n2", l, k), ("h_lo", "n2", l, k))
                        for s in ((1, 0) if t0 == 0 else (0,)):
                            cols = slice((1 - s) * TC, (1 - s) * TC + TC)
                            ins = dve.scalar_tensor_tensor(
                                r[:, cols], x[:, k, cols], amp[:, 1, k, s:s + 1],
                                given("rs", ("n2", l))[:, cols.start - t0:cols.stop - t0], ALU.mult, ALU.mult)
                        ins.then_inc(*signal("scaled", "n2", l, k))
                    if k:
                        v = k - 1
                        r = given("raw", ("n2", l, v))
                        dve.wait_ge(*event("h_hi", "n2", l, v))
                        for s in ((1, 0) if t0 == 0 else (0,)):
                            cols = slice((1 - s) * TC, (1 - s) * TC + TC)
                            ins = dve.scalar_tensor_tensor(h_parts[:, 1, v, cols], r[:, cols], mod(l, s)[:, 24 + v:25 + v],
                                                           h_parts[:, 0, v, cols].bitcast(F32), ALU.add, ALU.subtract)
                        ins.then_inc(*signal("h_lo", "n2", l, v))
                for g in range(NG):
                    for n in range(GT * g, GT * g + GT + 1):
                        if n < GT * g + GT:
                            split_weights(("ff1", l, n))
                            r = take(dve, "raw", ("ff", l, n), ("b_lo", "ff", l, g, n % GT))[:, t0:TT]
                            dve.wait_ge(*event("psum_full", "ff1", l, n))
                            dve.tensor_scalar(r, bank(("ff1", l, n))[:, 0:cw], 0.0, None, ALU.max).then_inc(*signal("relu", l, n))
                        if n > GT * g:
                            v = (n - 1) % GT
                            low_part(b_parts, v, given("raw", ("ff", l, n - 1))[:, t0:TT], slice(t0, TT), "b", "ff", l, g)
                    for n in range(KT):
                        split_weights(("ff2", l, g, n))
                        residual(n, 40, "x_mlp", "ff2", l, g, n)

            def norm3(l):
                dve.wait_ge(*event("rs", "n3", l))
                for k in range(KT):
                    dve.scalar_tensor_tensor(h2[:, k, :], x2[:, k, :], p("pre", l - L)[:, k:k + 1],
                                             given("rs", ("n3", l))[:, 0:T], ALU.mult, ALU.mult).then_inc(*signal("h2", l, k))

            def memory_gain(l):
                for k in range(KT):
                    dve.tensor_scalar(memn[:, k, :], mem[:, k, :], p("mem", l - L)[:, k:k + 1], None,
                                      ALU.mult).then_inc(*signal("memn", l, k))

            norm3(L)
            dve.wait_ge(*event("rs", "mem", 2))
            for k in range(KT):
                dve.tensor_tensor(mem[:, k, :], mem[:, k, :], given("rs", ("mem", 2))[:, 0:T],
                                  ALU.mult).then_inc(*signal("mem_normed", k))
            dve.wait_ge(*event("con2_in"))
            dve.wait_ge(*event("mem_normed", KT - 1))
            memory_gain(L)
            for lw in range(L):
                l = L + lw
                if lw:
                    norm3(l)
                dve.wait_ge(*event("psum_full", "dt", l))
                for t in range(2):
                    dve.tensor_tensor(delta[:, 0, 8 * t:8 * t + 8], bank(("dt", l))[:, 8 * t:8 * t + 8],
                                          p("dt_bias", lw), ALU.add).then_inc(*signal("dt_bias", l, t))
                dve.wait_ge(*event("dt_bias", l, 1))
                dve.scalar_tensor_tensor(delta[:, 1, :], delta[:, 0, :], -1.0, delta[:, 0, :], ALU.mult, ALU.min).then_inc(*signal("dt_abs", l))

                def conv_silu(i):
                    e = given("tmp", ("conv", l, i))[:, 0:T]
                    dve.wait_ge(*event("conv_exp", l, i))
                    sigmoid(e)
                    dve.tensor_tensor(xbc[:, i, :], xbc[:, i, :], e, ALU.mult).then_inc(*signal("xbc", l, i))

                for i in range(9):
                    if i < 8:
                        dve.wait_ge(*event("psum_full", "xbc", l, i))
                        dve.tensor_copy(conv_in[:, i, :], bank(("xbc", l, i))[:, 0:T]).then_inc(*signal("copied", "xbc", l, i))
                        dve.wait_ge(*event("copied", "xbc", l, i))
                        taps = p("conv_w", lw)[:, 4 * i:4 * i + 4]
                        then(dve.tensor_scalar(xbc[:, i, :], conv_in[:, i, :], taps[:, 3:4],
                                               p("conv_b", lw)[:, i:i + 1], ALU.mult, ALU.add))
                        for j in range(1, 4):
                            ins = dve.scalar_tensor_tensor(xbc[:, i, j:T], conv_in[:, i, 0:T - j], taps[:, 3 - j:4 - j],
                                                           xbc[:, i, j:T], ALU.mult, ALU.add)
                            then(ins) if j < 3 else ins.then_inc(*signal("conv", l, i))
                    if i:
                        conv_silu(i - 1)
                for name in ("rq", "rk"):
                    for i in range(4):
                        ps = bank((name, l, i))
                        e = rope_tmp[:, i % 2, :]
                        dve.wait_ge(*event("psum_full", name, l, i))
                        dve.tensor_tensor(e[0:64, :], ps[64:P, 0:T], c2("sin")[64:P, :], ALU.mult)
                        dve.tensor_tensor(e[64:P, :], ps[0:64, 0:T], c2("sin")[0:64, :], ALU.mult)
                        then(dve.tensor_tensor(heads2[name][:, i, :], ps[:, 0:T], c2("cos"), ALU.mult))
                        dve.tensor_tensor(heads2[name][:, i, :], heads2[name][:, i, :], e, ALU.add).then_inc(*signal("roped", name, l, i))
                dve.wait_ge(*event("dt_log", l))
                then(dve.scalar_tensor_tensor(delta[:, 1, :], delta[:, 0, :], 0.0, delta[:, 3, :], ALU.max, ALU.add))
                dve.wait_ge(*event("a_exp", l))
                for t in range(2):
                    then(dve.scalar_tensor_tensor(delta[:, 4, 8 * t:8 * t + 8], delta[:, 1, 8 * t:8 * t + 8], -1.0,
                                                  delta[:, 5, 0:8], ALU.mult, ALU.mult))
                def gate_silu(n):
                    i = GATES[n]
                    e = given("tmp", ("gate", l, i))[:, 0:T]
                    dve.wait_ge(*event("gate_exp2", l, i))
                    sigmoid(e)
                    dve.tensor_tensor(gate[:, i, :], e, bank(("gate", l, i))[:, 0:T], ALU.mult).then_inc(*signal("gated_in", "gate", l, i))

                for g in range(2):
                    dve.wait_ge(*event("psum_full", "cb", l, g))
                    dve.tensor_tensor(cbm[:, g, :], bank(("cb", l, g))[:, 0:W2], c2("causal"), ALU.mult).then_inc(*signal("cb_masked", l, g))

                def ssd_du(hd):
                    if hd >= 2:
                        dve.wait_ge(*event("psum_full", "seg", l, hd - 2))
                    b = hd % 2
                    dve.tensor_scalar(du[:, b, 0:P], c2("gt"), delta[:, 4, hd:hd + 1], None, ALU.mult)
                    dve.tensor_scalar(du[:, b, P:2 * P], ones, delta[:, 4, 8 + hd:9 + hd], None, ALU.mult)
                    dve.tensor_scalar(du[:, b, 2 * P:W2], c2("gt"), delta[:, 4, 8 + hd:9 + hd], None, ALU.mult).then_inc(*signal("du", l, hd))

                def ssd_y(j):
                    dve.wait_ge(*event("psum_full", "ssdY", l, j))
                    dve.scalar_tensor_tensor(y2(4 + j), xbc[:, j, :], p("d_skip", lw)[:, j:j + 1],
                                                 bank(("ssdY", l, j))[:, 0:T], ALU.mult, ALU.add).then_inc(*signal("ssd_skip", l, j))
                    dve.wait_ge(*event("ssd_skip", l, j))
                    dve.tensor_tensor(y2(4 + j), y2(4 + j), gate[:, 4 + j, :], ALU.mult).then_inc(*signal("ssd_gated", l, j))

                dve.wait_ge(*event("cb_masked", l, 1))
                ssd_du(0)
                ssd_du(1)
                for hd in range(8):
                    e = given("tmp", ("ssd_g", l, hd))
                    dve.wait_ge(*event("seg_exp", l, hd))
                    g = hd // 4
                    dve.scalar_tensor_tensor(e[:, 0:T], e[:, 0:T], delta[:, 1, hd:hd + 1], cbm[:, g, 0:T],
                                             ALU.mult, ALU.mult)
                    dve.scalar_tensor_tensor(e[:, T:W2], e[:, T:W2], delta[:, 1, 8 + hd:9 + hd], cbm[:, g, T:W2],
                                                 ALU.mult, ALU.mult).then_inc(*signal("ssd_g", l, hd))
                    if hd + 2 < 8:
                        ssd_du(hd + 2)
                    gate_silu(hd)
                    if hd % 2 == 0 and hd:
                        ssd_y(hd // 2 - 1)
                ssd_y(3)
                for g in range(2):
                    dve.wait_ge(*event("rs", ("ssd", g), l))
                    for k in range(2):
                        j = 2 * g + k
                        dve.scalar_tensor_tensor(y2(4 + j), y2(4 + j), p("ssd", lw)[:, j:j + 1],
                                                     given("rs", (("ssd", g), l))[:, 0:T], ALU.mult, ALU.mult).then_inc(*signal("gated", l, 4 + j))

                for hd in range(5):
                    if hd < 4:
                        e = take(dve, "work", ("ret_decay", l, hd), ("psum_full", "retY", l, hd))
                        dve.wait_ge(*event("psum_full", "retS", l, hd))
                        dve.tensor_tensor(e[:, 0:W2], bank(("retS", l, hd))[:, 0:W2],
                                              c2("decay")[:, W2 * hd:W2 * hd + W2], ALU.mult).then_inc(*signal("ret_decay", l, hd))
                        gate_silu(8 + hd)
                    if hd:
                        dve.wait_ge(*event("psum_full", "retY", l, hd - 1))
                        dve.tensor_copy(y2(hd - 1), bank(("retY", l, hd - 1))[:, 0:T]).then_inc(*signal("ret_y", l, hd - 1))
                for hd in range(4):
                    dve.wait_ge(*event("psum_full", "retM", l, hd))
                    dve.scalar_tensor_tensor(y2(hd), bank(("retM", l, hd))[:, 0:T], -1.0 / P, y2(hd),
                                                 ALU.mult, ALU.add).then_inc(*signal("ret_centre", l, hd))
                for hd in range(4):
                    dve.wait_ge(*event("rs", ("ret", hd), l))
                    dve.wait_ge(*event("squared", ("ret", hd), l, 0))
                    then(dve.tensor_tensor(y2(hd), y2(hd), given("rs", (("ret", hd), l))[:, 0:T], ALU.mult))
                    dve.tensor_tensor(y2(hd), y2(hd), gate[:, hd, :], ALU.mult).then_inc(*signal("gated", l, hd))

                for hd in range(7):
                    if hd < 4:
                        z = take(dve, "work", ("sb_logit", l, hd), ("psum_full", "sbY", l, hd))[:, 0:W2]
                        dve.wait_ge(*event("psum_full", "sbS", l, hd))
                        dve.tensor_scalar(z, bank(("sbS", l, hd))[:, 0:W2], float(P) ** -0.5, None,
                                          ALU.mult).then_inc(*signal("sb_logit", l, hd))
                        dve.wait_ge(*event("sb_logit", l, hd))
                        s2 = take(dve, "sb_abs", (l, hd), ("sb_log", l, hd))
                        dve.scalar_tensor_tensor(s2, z, -1.0, z, ALU.mult, ALU.min).then_inc(*signal("sb_abs", l, hd))
                    if 0 < hd < 5:
                        v = hd - 1
                        z = given("work", ("sb_logit", l, v))[:, 0:W2]
                        s = given("sq", ("sb", l, v))[:, 0:W2]
                        dve.wait_ge(*event("sb_log", l, v))
                        then(dve.scalar_tensor_tensor(s, z, 0.0, s, ALU.max, ALU.add))
                        dve.tensor_tensor(s, s, c2("strict"), ALU.mult).then_inc(*signal("sb_softplus", l, v))
                        gate_silu(12 + v)
                    if 1 < hd < 6:
                        v = hd - 2
                        z = given("work", ("sb_logit", l, v))[:, 0:W2]
                        dve.wait_ge(*event("psum_full", "sbT", l, v))
                        then(dve.scalar_tensor_tensor(z, bank(("sbT", l, v))[:, 0:W2], -1.0, z, ALU.mult, ALU.add))
                        dve.tensor_tensor(z, z, c2("neg"), ALU.add).then_inc(*signal("sb_tail", l, v))
                    if hd > 2:
                        v = hd - 3
                        dve.wait_ge(*event("psum_full", "sbY", l, v))
                        dve.tensor_tensor(y2(8 + v), bank(("sbY", l, v))[:, 0:T], gate[:, 8 + v, :],
                                          ALU.mult).then_inc(*signal("gated", l, 8 + v))

                def y_out(hd):
                    dve.wait_ge(*event("psum_full", ("memory", l), "Y", hd))
                    dve.tensor_tensor(y2(12 + hd), bank((("memory", l), "Y", hd))[:, 0:T], gate[:, 12 + hd, :],
                                          ALU.mult).then_inc(*signal("mem_gated", ("memory", l), hd))

                softmax(("memory", l), 8, T, False, y_out)

                for n in range(KT):
                    dve.wait_ge(*event("psum_full", "out2", l, n))
                    dve.tensor_copy(yo[:, n, :], bank(("out2", l, n))[:, 0:T]).then_inc(*signal("out_copied", l, n))
                if l < 2 * L - 1:
                    memory_gain(l + 1)
                dve.wait_ge(*event("rs", "n4", l))
                for k in range(KT):
                    then(dve.scalar_tensor_tensor(yo[:, k, :], yo[:, k, :], p("post", lw)[:, k:k + 1],
                                                  given("rs", ("n4", l))[:, 0:T], ALU.mult, ALU.mult))
                    dve.tensor_tensor(x2[:, k, :], x2[:, k, :], yo[:, k, :], ALU.add).then_inc(*signal("x_out", l, k))
    return seen


def lay_out(a):
    def cols(v):
        v = np.asarray(v, np.float32)
        return v.reshape(-1, P).T

    def pad(v):
        out = np.zeros((P, v.shape[0]), np.float32)
        out[:v.shape[1]] = v.T
        return out

    def feature_major(v):
        return np.ascontiguousarray(v.T.reshape(KT, P, -1).transpose(1, 0, 2))

    chunks, _ = weight_chunks()
    parts = []
    for entries, size in chunks:
        parts.append(np.concatenate([
            a[src][l, k0:k0 + P * nk][:, list(cc)].reshape(nk, P, len(cc)).transpose(1, 0, 2).reshape(P, -1)
            for _, src, l, k0, nk, cc in entries], axis=1).ravel())
    w = np.concatenate(parts)

    cvec = np.stack([a["c"][0], a["c_ctx"]])
    two = lambda v: np.concatenate([v, v], axis=1).T
    params = {
        "c": cvec.reshape(2, KT, P).transpose(2, 1, 0).reshape(P, -1),
        "b_ada": cols(a["b_ada"]), "g_attn": cols(a["g_attn"]), "g_mlp": cols(a["g_mlp"]),
        "g_qa": cols(a["g_qa"]), "g_kva": cols(a["g_kva"]), "g_mla_q": pad(a["g_mla_q"]),
        "g_mla_k": pad(a["g_mla_k"]), "g_na_q": two(a["g_na_q"]), "g_na_k": two(a["g_na_k"]),
        "pre": cols(a["pre_norm_g_2"]), "post": cols(a["post_norm_g_2"]), "mem": cols(a["mem_norm_g_2"]),
        "ssd": cols(a["ssd_norm_g_2"]),
        "conv_w": a["conv_w_2"].reshape(L, 4, 8, P).transpose(3, 0, 2, 1).reshape(P, -1),
        "conv_b": cols(a["conv_b_2"]), "d_skip": cols(np.repeat(a["d_skip_2"], 64, axis=1)),
        "dt_bias": np.broadcast_to(a["dt_bias_2"].reshape(1, -1), (P, 16)),
        "a_log": np.broadcast_to(a["a_log_2"].reshape(1, -1), (P, 16))}
    par = np.zeros((P, NPARAMS), np.float32)
    for name, v in params.items():
        par[:, PARAMS[name][0]:PARAMS[name][1]] = v

    rows = T // GRID
    q, k = np.arange(T)[:, None], np.arange(T)[None, :]
    qr, qc, kr, kc = q // GRID, q % GRID, k // GRID, k % GRID
    kh = min(KH, rows)
    r_start = np.clip(qr - kh // 2, 0, rows - kh)
    c_start = np.clip(qc - KW // 2, 0, GRID - KW)
    inside = (kr >= r_start) & (kr < r_start + kh) & (kc >= c_start) & (kc < c_start + KW)
    dr = np.clip(kr - qr + KH - 1, 0, 2 * KH - 2)
    dc = np.clip(kc - qc + KW - 1, 0, 2 * KW - 2)
    bias = np.where(inside, a["rpb"][:, :, dr, dc], np.float32(NEG))
    bias = np.ascontiguousarray(bias.reshape(L, NH, 2, P, T).transpose(0, 3, 2, 1, 4)).astype(np.float32)
    return {"w": w, "par": par, "bias": bias, "mem": feature_major(a["mem_2"][0]),
            "x": feature_major(np.concatenate([a["ctx"][0], a["x"][0]])), **constants()}


def constants():
    i = np.arange(P)
    con = np.zeros((P, NCONST), np.float32)
    put = lambda arr, table, name, v, r=slice(0, P): arr.__setitem__((r, slice(*table[name])), v)
    put(con, CONST, "ident", np.eye(P))
    put(con, CONST, "ones", 1.0)
    put(con, CONST, "pair", (i[:, None] // 64 == i[None, :] // 64))
    rot = np.zeros((ROPE, ROPE))
    for b in (0, 16):
        for m in range(8):
            rot[b + m + 8, b + m] = -1.0
            rot[b + m, b + m + 8] = 1.0
    put(con, CONST, "rot", rot, slice(NOPE, QK))
    put(con, CONST, "eps", EPS)
    put(con, CONST, "one", 1.0)
    t = np.arange(T)
    inv = (10000.0 ** (-np.arange(8, dtype=np.float32) / 8)).astype(np.float32)
    row = (t // GRID).astype(np.float32)[None, :] * inv[:, None]
    col = (t % GRID).astype(np.float32)[None, :] * inv[:, None]
    ang = np.concatenate([row, row, col, col])
    put(con, CONST, "cos", np.cos(ang), slice(NOPE, QK))
    put(con, CONST, "sin", np.sin(ang), slice(NOPE, QK))

    con2 = np.zeros((P, NCONST2), np.float32)
    causal_pair = lambda f: np.concatenate([f(i[:, None], t[None, :]), f(i[:, None] + P, t[None, P:])], axis=1)
    put(con2, CONST2, "gt", i[:, None] > i[None, :])
    put(con2, CONST2, "le", i[:, None] <= t[None, :])
    put(con2, CONST2, "ge", i[:, None] >= i[None, :])
    put(con2, CONST2, "causal", causal_pair(lambda s, l: s <= l))
    put(con2, CONST2, "strict", causal_pair(lambda s, l: s < l))
    put(con2, CONST2, "neg", causal_pair(lambda s, l: np.where(s < l, 0.0, NEG)))
    log_g = np.log(1.0 - 2.0 ** (-5.0 - np.arange(4)))
    put(con2, CONST2, "decay", np.concatenate([
        causal_pair(lambda s, l: np.where(s <= l, np.exp((l - s) * g), 0.0) * P ** -0.5) for g in log_g], axis=1))
    inv = (10000.0 ** (-np.arange(0, P, 2, dtype=np.float32) / P)).astype(np.float32)
    ang = t.astype(np.float32)[None, :] * inv[:, None]
    put(con2, CONST2, "cos", np.concatenate([np.cos(ang), np.cos(ang)]))
    put(con2, CONST2, "sin", np.concatenate([np.sin(ang), -np.sin(ang)]))
    return {"con": con, "con2": con2}


def kernel(**inputs):
    import concourse.bacc as bacc
    from concourse.bass_utils import run_bass_kernel_spmd

    arrays = lay_out({k: np.asarray(v) for k, v in inputs.items()})

    def build(numbers):
        nc = bacc.Bacc("TRN2", target_bir_lowering=False, num_devices=1)
        dram = {n: nc.dram_tensor(f"in_{n}", v.shape, F32, kind="ExternalInput").ap() for n, v in arrays.items()}
        dram["out"] = nc.dram_tensor("out_0", (P, KT, T), F32, kind="ExternalOutput").ap()
        return nc, program(nc, dram, numbers)

    _, numbers = build({})
    nc, again = build(numbers)
    assert again == numbers
    r = run_bass_kernel_spmd(nc, [{f"in_{n}": v for n, v in arrays.items()}], core_ids=[0])
    out = r.results[0]["out_0"]
    return np.ascontiguousarray(out.transpose(2, 1, 0).reshape(1, T, D))
```
